# Optimizing a Trainium2 kernel written in Bass

```python
import math
import jax, jax.numpy as jnp
from jax import lax
import numpy as np

D_MODEL = 1024
BATCH = 1
SEQ = 256
DEPTH = 2

GRID_W = 64
HEAD_DIM = 128
ATTN_WIDTH = D_MODEL
N_HEADS = ATTN_WIDTH // HEAD_DIM
N_KV_HEADS = 2
GROUP = N_HEADS // N_KV_HEADS
KV_WIDTH = N_KV_HEADS * HEAD_DIM
Q_BLOCK = 128
ROPE_THETA = 10000.0
ROPE_HALF = HEAD_DIM // 2
POOL_WINDOWS = (2, 4, 8, 16)
N_POOL_GROUPS = 4
POOL_WIDTH = D_MODEL // 2
POOL_GROUP_DIM = POOL_WIDTH // N_POOL_GROUPS
IN_COLS = ATTN_WIDTH + 2 * KV_WIDTH + POOL_WIDTH + 2 * D_MODEL
N_PEER_HEADS = 8
PEER_QUERY_DIM = 512
SUBKEY_DIM = PEER_QUERY_DIM // 2
N_KEYS = 128
N_EXPERTS = N_KEYS * N_KEYS
PEER_TOPK = 16
TOKEN_BLOCK = 128
N_ADA = 6
EPS = 1e-6


def rms_norm(x, w):
    xf = x.astype(jnp.float32)
    y = xf * lax.rsqrt(jnp.mean(xf * xf, axis=-1, keepdims=True) + EPS)
    return (y * w.astype(jnp.float32)).astype(x.dtype)

def modulate(xn, shift, scale):
    return xn * (1.0 + scale[:, None, :]) + shift[:, None, :]

def axial_rope_angles(seq_len):
    rows = seq_len // GRID_W
    t = jnp.arange(rows * GRID_W)
    row = (t // GRID_W).astype(jnp.float32)
    col = (t % GRID_W).astype(jnp.float32)
    inv = 1.0 / (ROPE_THETA ** (jnp.arange(0, ROPE_HALF, 2, dtype=jnp.float32) / ROPE_HALF))
    return row[:, None] * inv, col[:, None] * inv

def rotate_half_dims(xh, ang):
    half = ROPE_HALF // 2
    cos = jnp.cos(ang)[None, :, None, :]
    sin = jnp.sin(ang)[None, :, None, :]
    xf = xh.astype(jnp.float32)
    x1, x2 = xf[..., :half], xf[..., half:]
    return jnp.concatenate([x1 * cos - x2 * sin, x2 * cos + x1 * sin], axis=-1).astype(xh.dtype)

def apply_axial_rope(x, ang_r, ang_c):
    return jnp.concatenate([rotate_half_dims(x[..., :ROPE_HALF], ang_r),
                            rotate_half_dims(x[..., ROPE_HALF:], ang_c)], axis=-1)

def blocked_bidirectional_gqa(q, k, v):
    B, S = q.shape[0], q.shape[1]
    nb = S // Q_BLOCK
    scale = 1.0 / math.sqrt(HEAD_DIM)
    qb = q.reshape(B, nb, Q_BLOCK, N_KV_HEADS, GROUP, HEAD_DIM).swapaxes(0, 1)

    def one_block(qblk):
        s = jnp.einsum('bqkgd,bskd->bkgqs', qblk, k).astype(jnp.float32) * scale
        p = jax.nn.softmax(s, axis=-1).astype(v.dtype)
        return jnp.einsum('bkgqs,bskd->bqkgd', p, v)

    ob = lax.map(one_block, qb)
    return ob.swapaxes(0, 1).reshape(B, S, N_HEADS * HEAD_DIM)

def multiscale_pool(u, pool_mix_w, pool_scale):
    B, S, _ = u.shape
    ug = u.reshape(B, S, N_POOL_GROUPS, POOL_GROUP_DIM).astype(jnp.float32)
    t = jnp.arange(S)
    outs = []
    for gi, w in enumerate(POOL_WINDOWS):
        xg = ug[:, :, gi, :]
        csum = jnp.concatenate([jnp.zeros((B, 1, POOL_GROUP_DIM), jnp.float32),
                                jnp.cumsum(xg, axis=1)], axis=1)
        lo = jnp.clip(t - w // 2, 0, S)
        hi = jnp.clip(t + w // 2, 0, S)
        cnt = (hi - lo).astype(jnp.float32)[None, :, None]
        outs.append((csum[:, hi] - csum[:, lo]) / cnt - xg)
    m = jnp.stack(outs, axis=2).astype(u.dtype)
    mixed = jnp.einsum('bsgc,gcd->bsgd', m, pool_mix_w).reshape(B, S, POOL_WIDTH)
    return mixed * pool_scale

def peer_ffn(xm, w_query, sub_keys, expert_u, expert_v):
    B, S, D = xm.shape
    nb = S // TOKEN_BLOCK
    xb = xm.reshape(B, nb, TOKEN_BLOCK, D).swapaxes(0, 1)

    def one_block(xblk):
        q = (xblk @ w_query).reshape(B, TOKEN_BLOCK, N_PEER_HEADS, 2, SUBKEY_DIM)
        s = jnp.einsum('bthpd,hpnd->bthpn', q, sub_keys).astype(jnp.float32)
        vals, idx = lax.top_k(s, PEER_TOPK)
        cand = (vals[..., 0, :, None] + vals[..., 1, None, :]).reshape(B, TOKEN_BLOCK, N_PEER_HEADS, PEER_TOPK * PEER_TOPK)
        cand_idx = (idx[..., 0, :, None] * N_KEYS + idx[..., 1, None, :]).reshape(B, TOKEN_BLOCK, N_PEER_HEADS, PEER_TOPK * PEER_TOPK)
        top_s, pos = lax.top_k(cand, PEER_TOPK)
        eidx = jnp.take_along_axis(cand_idx, pos, axis=-1)
        g = jax.nn.softmax(top_s, axis=-1).astype(xblk.dtype)
        u = expert_u[eidx]
        h = jnp.einsum('btd,bthkd->bthk', xblk, u)
        act = jax.nn.gelu(h, approximate=False) * g
        return jnp.einsum('bthk,bthkd->btd', act, expert_v[eidx])

    yb = lax.map(one_block, xb)
    return yb.swapaxes(0, 1).reshape(B, S, D)

def first_inputs(seed: int = 0) -> dict:
    key = jax.random.key(seed)
    ks = jax.random.split(key, 20)
    f32 = jnp.float32
    nrm = lambda k, shape, s: (jax.random.normal(k, shape, f32) * s)
    return {
        "x": nrm(ks[0], (BATCH, SEQ, D_MODEL), 1.0),
        "c": nrm(ks[1], (BATCH, D_MODEL), 1.0),
        "ada_w": nrm(ks[2], (DEPTH, D_MODEL, N_ADA * D_MODEL), 0.5 * D_MODEL ** -0.5),
        "ada_b": nrm(ks[3], (DEPTH, N_ADA * D_MODEL), 0.01),
        "norm_mix_w": 1.0 + nrm(ks[4], (DEPTH, D_MODEL), 0.05),
        "w_in": nrm(ks[5], (DEPTH, D_MODEL, IN_COLS), D_MODEL ** -0.5),
        "q_norm_w": 1.0 + nrm(ks[6], (DEPTH, HEAD_DIM), 0.05),
        "k_norm_w": 1.0 + nrm(ks[7], (DEPTH, HEAD_DIM), 0.05),
        "w_attn_o": nrm(ks[8], (DEPTH, ATTN_WIDTH, D_MODEL), ATTN_WIDTH ** -0.5),
        "pool_mix_w": nrm(ks[9], (DEPTH, N_POOL_GROUPS, POOL_GROUP_DIM, POOL_GROUP_DIM), POOL_GROUP_DIM ** -0.5),
        "pool_scale": 1.0 + nrm(ks[10], (DEPTH, POOL_WIDTH), 0.05),
        "w_pool_o": nrm(ks[11], (DEPTH, POOL_WIDTH, D_MODEL), POOL_WIDTH ** -0.5),
        "w_out": nrm(ks[12], (DEPTH, D_MODEL, D_MODEL), D_MODEL ** -0.5),
        "norm_ffn_w": 1.0 + nrm(ks[13], (DEPTH, D_MODEL), 0.05),
        "w_query": nrm(ks[14], (DEPTH, D_MODEL, N_PEER_HEADS * PEER_QUERY_DIM), D_MODEL ** -0.5),
        "sub_keys": nrm(ks[15], (DEPTH, N_PEER_HEADS, 2, N_KEYS, SUBKEY_DIM), SUBKEY_DIM ** -0.5),
        "expert_u": nrm(ks[16], (DEPTH, N_EXPERTS, D_MODEL), D_MODEL ** -0.5),
        "expert_v": nrm(ks[17], (DEPTH, N_EXPERTS, D_MODEL), N_PEER_HEADS ** -0.5),
        "final_norm_w": 1.0 + nrm(ks[18], (D_MODEL,), 0.05),
    }

def first_block(x, c, ada_w, ada_b, norm_mix_w, w_in, q_norm_w, k_norm_w, w_attn_o, pool_mix_w,
              pool_scale, w_pool_o, w_out, norm_ffn_w, w_query, sub_keys, expert_u, expert_v,
              final_norm_w):
    B, S, _ = x.shape
    ang_r, ang_c = axial_rope_angles(S)
    c_act = jax.nn.silu(c)
    splits = [ATTN_WIDTH, ATTN_WIDTH + KV_WIDTH, ATTN_WIDTH + 2 * KV_WIDTH,
              ATTN_WIDTH + 2 * KV_WIDTH + POOL_WIDTH, ATTN_WIDTH + 2 * KV_WIDTH + POOL_WIDTH + D_MODEL]
    for l in range(DEPTH):
        mod = c_act @ ada_w[l] + ada_b[l]
        sh1, sc1, g1, sh2, sc2, g2 = jnp.split(mod, N_ADA, axis=-1)

        xm = modulate(rms_norm(x, norm_mix_w[l]), sh1, sc1)
        proj = xm @ w_in[l]
        q, k, v, u_pool, ga, gp = jnp.split(proj, splits, axis=-1)

        q = rms_norm(q.reshape(B, S, N_HEADS, HEAD_DIM), q_norm_w[l])
        k = rms_norm(k.reshape(B, S, N_KV_HEADS, HEAD_DIM), k_norm_w[l])
        v = v.reshape(B, S, N_KV_HEADS, HEAD_DIM)
        q = apply_axial_rope(q, ang_r, ang_c).reshape(B, S, N_KV_HEADS, GROUP, HEAD_DIM)
        k = apply_axial_rope(k, ang_r, ang_c)
        attn = blocked_bidirectional_gqa(q, k, v) @ w_attn_o[l]

        pool = multiscale_pool(u_pool, pool_mix_w[l], pool_scale[l]) @ w_pool_o[l]

        merged = jax.nn.sigmoid(ga) * attn + jax.nn.sigmoid(gp) * pool
        x = x + g1[:, None, :] * (merged @ w_out[l])

        xf = modulate(rms_norm(x, norm_ffn_w[l]), sh2, sc2)
        x = x + g2[:, None, :] * peer_ffn(xf, w_query[l], sub_keys[l], expert_u[l], expert_v[l])

    return rms_norm(x, final_norm_w)


DEPTH_2 = 4

N_MIXERS = 3
HEAD_DIM_2 = 64
ROT_DIM = HEAD_DIM_2 // 4
ROPE_THETA_2 = 500000.0
NORM_EPS = 1e-6
D_FF = 4 * D_MODEL

DIFF_HEADS = D_MODEL // (2 * HEAD_DIM_2)
DIFF_QK_WIDTH = DIFF_HEADS * 2 * HEAD_DIM_2
DIFF_V_DIM = 2 * HEAD_DIM_2
DIFF_IN = 2 * DIFF_QK_WIDTH + DIFF_HEADS * DIFF_V_DIM
DENSE_Q_BLOCK = 128

MOBA_HEADS = D_MODEL // HEAD_DIM_2
MOBA_BLOCK = 256
MOBA_TOPK = 3
MOBA_Q_CHUNK = 32
MOBA_IN = 3 * MOBA_HEADS * HEAD_DIM_2

SWA_HEADS = D_MODEL // HEAD_DIM_2
SWA_KV_HEADS = SWA_HEADS // 8
SWA_WINDOW = 128
SWA_Q_BLOCK = SWA_WINDOW
SWA_IN = (SWA_HEADS + 2 * SWA_KV_HEADS) * HEAD_DIM_2

N_DIFF = (DEPTH_2 + 2) // 3
N_MOBA = (DEPTH_2 + 1) // 3
N_SWA = DEPTH_2 // 3


def rms_norm_2(x, g):
    xf = x.astype(jnp.float32)
    y = xf * lax.rsqrt(jnp.mean(xf * xf, axis=-1, keepdims=True) + NORM_EPS)
    return (y * g.astype(jnp.float32)).astype(x.dtype)

def rope_tables(positions):
    inv = ROPE_THETA_2 ** (-jnp.arange(0, ROT_DIM, 2, dtype=jnp.float32) / ROT_DIM)
    ang = positions.astype(jnp.float32)[..., None] * inv
    return jnp.cos(ang), jnp.sin(ang)

def apply_partial_rope(x, cos, sin):
    half = ROT_DIM // 2
    c = cos[:, :, None, :].astype(x.dtype)
    s = sin[:, :, None, :].astype(x.dtype)
    x1 = x[..., :half]
    x2 = x[..., half:ROT_DIM]
    return jnp.concatenate([x1 * c - x2 * s, x2 * c + x1 * s, x[..., ROT_DIM:]], axis=-1)

def diff_attention(h, w_in, w_out, lam_q1, lam_k1, lam_q2, lam_k2, sub_g, cos, sin, lambda_init):
    B, S, _ = h.shape
    H = DIFF_HEADS
    qkv = h @ w_in
    q, k, v = jnp.split(qkv, [DIFF_QK_WIDTH, 2 * DIFF_QK_WIDTH], axis=-1)
    q = apply_partial_rope(q.reshape(B, S, 2 * H, HEAD_DIM_2), cos, sin) * (HEAD_DIM_2 ** -0.5)
    k = apply_partial_rope(k.reshape(B, S, 2 * H, HEAD_DIM_2), cos, sin)
    q = q.reshape(B, S, H, 2, HEAD_DIM_2)
    k = k.reshape(B, S, H, 2, HEAD_DIM_2)
    v = v.reshape(B, S, H, DIFF_V_DIM)
    f32 = jnp.float32
    lam = (jnp.exp(jnp.sum(lam_q1.astype(f32) * lam_k1.astype(f32)))
           - jnp.exp(jnp.sum(lam_q2.astype(f32) * lam_k2.astype(f32))) + lambda_init)
    nqb = S // DENSE_Q_BLOCK
    qb = q.reshape(B, nqb, DENSE_Q_BLOCK, H, 2, HEAD_DIM_2).transpose(1, 0, 2, 3, 4, 5)
    key_pos = jnp.arange(S)

    def block(args):
        qi, blk = args
        q_pos = blk * DENSE_Q_BLOCK + jnp.arange(DENSE_Q_BLOCK)
        s = jnp.einsum('bqhcd,bkhcd->bhcqk', qi, k).astype(f32)
        causal = key_pos[None, :] <= q_pos[:, None]
        s = jnp.where(causal, s, -jnp.inf)
        p = jax.nn.softmax(s, axis=-1)
        p = p[:, :, 0] - lam * p[:, :, 1]
        return jnp.einsum('bhqk,bkhe->bqhe', p.astype(v.dtype), v)

    o = lax.map(block, (qb, jnp.arange(nqb)))
    o = o.transpose(1, 0, 2, 3, 4).reshape(B, S, H, DIFF_V_DIM)
    o = rms_norm_2(o, sub_g) * (1.0 - lambda_init)
    return o.reshape(B, S, H * DIFF_V_DIM) @ w_out

def moba_attention(h, w_in, w_out, cos, sin):
    B, S, _ = h.shape
    H, D, Bk = MOBA_HEADS, HEAD_DIM_2, MOBA_BLOCK
    f32 = jnp.float32
    q, k, v = jnp.split(h @ w_in, 3, axis=-1)
    q = apply_partial_rope(q.reshape(B, S, H, D), cos, sin) * (D ** -0.5)
    k = apply_partial_rope(k.reshape(B, S, H, D), cos, sin)
    v = v.reshape(B, S, H, D)
    nb = -(-S // Bk)
    pad = nb * Bk - S
    k = jnp.pad(k, ((0, 0), (0, pad), (0, 0), (0, 0)))
    v = jnp.pad(v, ((0, 0), (0, pad), (0, 0), (0, 0)))
    K = min(MOBA_TOPK, nb)
    kb = k.reshape(B, nb, Bk, H, D).transpose(0, 3, 1, 2, 4)
    vb = v.reshape(B, nb, Bk, H, D).transpose(0, 3, 1, 2, 4)
    k_mean = jnp.mean(kb.astype(f32), axis=3).astype(k.dtype)
    nqc = S // MOBA_Q_CHUNK
    qc = q.reshape(B, nqc, MOBA_Q_CHUNK, H, D).transpose(1, 0, 3, 2, 4)
    b_idx = jnp.arange(B)[:, None, None, None]
    h_idx = jnp.arange(H)[None, :, None, None]
    blk_ids = jnp.arange(nb)
    in_blk = jnp.arange(Bk)

    def chunk(args):
        qi, ci = args
        q_pos = ci * MOBA_Q_CHUNK + jnp.arange(MOBA_Q_CHUNK)
        own = (ci * MOBA_Q_CHUNK) // Bk
        gate = jnp.einsum('bhqd,bhnd->bhqn', qi, k_mean).astype(f32)
        gate = jnp.where(blk_ids < own, gate, -jnp.inf)
        _, sel = lax.top_k(gate, K)
        valid = jnp.arange(K) < own
        ks = kb[b_idx, h_idx, sel]
        vs = vb[b_idx, h_idx, sel]
        s_sel = jnp.einsum('bhqd,bhqnkd->bhqnk', qi, ks).astype(f32)
        s_sel = jnp.where(valid[:, None], s_sel, -jnp.inf).reshape(B, H, MOBA_Q_CHUNK, K * Bk)
        k_own = lax.dynamic_index_in_dim(kb, own, axis=2, keepdims=False)
        v_own = lax.dynamic_index_in_dim(vb, own, axis=2, keepdims=False)
        s_own = jnp.einsum('bhqd,bhkd->bhqk', qi, k_own).astype(f32)
        own_pos = own * Bk + in_blk
        s_own = jnp.where(own_pos[None, :] <= q_pos[:, None], s_own, -jnp.inf)
        p = jax.nn.softmax(jnp.concatenate([s_sel, s_own], axis=-1), axis=-1).astype(v.dtype)
        p_sel = p[..., :K * Bk].reshape(B, H, MOBA_Q_CHUNK, K, Bk)
        p_own = p[..., K * Bk:]
        return (jnp.einsum('bhqnk,bhqnkd->bhqd', p_sel, vs)
                + jnp.einsum('bhqk,bhkd->bhqd', p_own, v_own))

    o = lax.map(chunk, (qc, jnp.arange(nqc)))
    o = o.transpose(1, 0, 3, 2, 4).reshape(B, S, H * D)
    return o @ w_out

def swa_sink_attention(h, w_in, b_in, sinks, w_out, cos, sin):
    B, S, _ = h.shape
    KV, D, Qb = SWA_KV_HEADS, HEAD_DIM_2, SWA_Q_BLOCK
    G = SWA_HEADS // KV
    f32 = jnp.float32
    qkv = h @ w_in + b_in
    q, k, v = jnp.split(qkv, [SWA_HEADS * D, (SWA_HEADS + KV) * D], axis=-1)
    q = apply_partial_rope(q.reshape(B, S, SWA_HEADS, D), cos, sin) * (D ** -0.5)
    k = apply_partial_rope(k.reshape(B, S, KV, D), cos, sin)
    v = v.reshape(B, S, KV, D)
    nb = S // Qb
    qb = q.reshape(B, nb, Qb, KV, G, D)
    kb = k.reshape(B, nb, Qb, KV, D)
    vb = v.reshape(B, nb, Qb, KV, D)
    pad_k = jnp.zeros_like(kb[:, :1])
    pad_v = jnp.zeros_like(vb[:, :1])
    k2 = jnp.concatenate([jnp.concatenate([pad_k, kb[:, :-1]], axis=1), kb], axis=2)
    v2 = jnp.concatenate([jnp.concatenate([pad_v, vb[:, :-1]], axis=1), vb], axis=2)
    s = jnp.einsum('bnqkgd,bnjkd->bnkgqj', qb, k2).astype(f32)
    qi = jnp.arange(Qb)[:, None] + Qb
    kj = jnp.arange(2 * Qb)[None, :]
    dist = qi - kj
    band = (dist >= 0) & (dist < SWA_WINDOW)
    prev_ok = (jnp.arange(nb)[:, None] > 0) | (jnp.arange(2 * Qb)[None, :] >= Qb)
    mask = band[None, :, :] & prev_ok[:, None, :]
    s = jnp.where(mask[None, :, None, None], s, -jnp.inf)
    sink = sinks.astype(f32).reshape(KV, G)[None, None, :, :, None, None]
    m = jnp.maximum(jnp.max(s, axis=-1, keepdims=True), sink)
    e = jnp.exp(s - m)
    p = (e / (jnp.sum(e, axis=-1, keepdims=True) + jnp.exp(sink - m))).astype(v.dtype)
    o = jnp.einsum('bnkgqj,bnjkd->bnqkgd', p, v2).reshape(B, S, SWA_HEADS * D)
    return o @ w_out

def sqrelu_mlp(h, w_up, w_down):
    a = jnp.maximum(h @ w_up, 0)
    return (a * a) @ w_down

def second_inputs(seed: int = 0) -> dict:
    key = jax.random.key(seed)
    ks = jax.random.split(key, 24)
    f32 = jnp.float32
    nrm = lambda k, shape, scale: jax.random.normal(k, shape, f32) * scale
    x = jax.random.normal(ks[0], (BATCH, SEQ, D_MODEL), f32)
    positions = jnp.broadcast_to(jnp.arange(SEQ, dtype=jnp.int32)[None, :], (BATCH, SEQ))
    return {
        "x": x,
        "positions": positions,
        "attn_norm_g": 1.0 + nrm(ks[1], (DEPTH_2, D_MODEL), 0.02),
        "mlp_norm_g": 1.0 + nrm(ks[2], (DEPTH_2, D_MODEL), 0.02),
        "diff_w_in": nrm(ks[3], (N_DIFF, D_MODEL, DIFF_IN), D_MODEL ** -0.5),
        "diff_w_out": nrm(ks[4], (N_DIFF, DIFF_HEADS * DIFF_V_DIM, D_MODEL), (DIFF_HEADS * DIFF_V_DIM) ** -0.5),
        "diff_lam_q1": nrm(ks[5], (N_DIFF, HEAD_DIM_2), 0.1),
        "diff_lam_k1": nrm(ks[6], (N_DIFF, HEAD_DIM_2), 0.1),
        "diff_lam_q2": nrm(ks[7], (N_DIFF, HEAD_DIM_2), 0.1),
        "diff_lam_k2": nrm(ks[8], (N_DIFF, HEAD_DIM_2), 0.1),
        "diff_subln_g": 1.0 + nrm(ks[9], (N_DIFF, DIFF_V_DIM), 0.02),
        "moba_w_in": nrm(ks[10], (N_MOBA, D_MODEL, MOBA_IN), D_MODEL ** -0.5),
        "moba_w_out": nrm(ks[11], (N_MOBA, MOBA_HEADS * HEAD_DIM_2, D_MODEL), (MOBA_HEADS * HEAD_DIM_2) ** -0.5),
        "swa_w_in": nrm(ks[12], (N_SWA, D_MODEL, SWA_IN), D_MODEL ** -0.5),
        "swa_b_in": nrm(ks[13], (N_SWA, SWA_IN), 0.02),
        "swa_sinks": nrm(ks[14], (N_SWA, SWA_HEADS), 0.5),
        "swa_w_out": nrm(ks[15], (N_SWA, SWA_HEADS * HEAD_DIM_2, D_MODEL), (SWA_HEADS * HEAD_DIM_2) ** -0.5),
        "mlp_w_up": nrm(ks[16], (DEPTH_2, D_MODEL, D_FF), D_MODEL ** -0.5),
        "mlp_w_down": nrm(ks[17], (DEPTH_2, D_FF, D_MODEL), 0.5 * D_FF ** -0.5),
        "final_norm_g": 1.0 + nrm(ks[18], (D_MODEL,), 0.02),
    }

def second_block(x, positions, attn_norm_g, mlp_norm_g, diff_w_in, diff_w_out, diff_lam_q1, diff_lam_k1,
              diff_lam_q2, diff_lam_k2, diff_subln_g, moba_w_in, moba_w_out, swa_w_in, swa_b_in,
              swa_sinks, swa_w_out, mlp_w_up, mlp_w_down, final_norm_g):
    cos, sin = rope_tables(positions)
    h = x
    for i in range(DEPTH_2):
        mixer = i % N_MIXERS
        slot = i // N_MIXERS
        a = rms_norm_2(h, attn_norm_g[i])
        if mixer == 0:
            lambda_init = 0.8 - 0.6 * math.exp(-0.3 * i)
            y = diff_attention(a, diff_w_in[slot], diff_w_out[slot], diff_lam_q1[slot], diff_lam_k1[slot],
                               diff_lam_q2[slot], diff_lam_k2[slot], diff_subln_g[slot], cos, sin, lambda_init)
        elif mixer == 1:
            y = moba_attention(a, moba_w_in[slot], moba_w_out[slot], cos, sin)
        else:
            y = swa_sink_attention(a, swa_w_in[slot], swa_b_in[slot], swa_sinks[slot], swa_w_out[slot], cos, sin)
        h = h + y
        h = h + sqrelu_mlp(rms_norm_2(h, mlp_norm_g[i]), mlp_w_up[i], mlp_w_down[i])
    return rms_norm_2(h, final_norm_g)


def setup_inputs(seed=0):
    out = dict(first_inputs(seed))
    for name, value in second_inputs(seed + 1).items():
        if name != "x":
            out[name + "_2"] = value
    return out


def reference(
    x, c, ada_w, ada_b, norm_mix_w, w_in, q_norm_w, k_norm_w, w_attn_o, pool_mix_w, pool_scale,
    w_pool_o, w_out, norm_ffn_w, w_query, sub_keys, expert_u, expert_v, final_norm_w,
    positions_2, attn_norm_g_2, mlp_norm_g_2, diff_w_in_2, diff_w_out_2, diff_lam_q1_2,
    diff_lam_k1_2, diff_lam_q2_2, diff_lam_k2_2, diff_subln_g_2, moba_w_in_2, moba_w_out_2,
    swa_w_in_2, swa_b_in_2, swa_sinks_2, swa_w_out_2, mlp_w_up_2, mlp_w_down_2, final_norm_g_2,
):
    x = first_block(
        x, c, ada_w, ada_b, norm_mix_w, w_in, q_norm_w, k_norm_w, w_attn_o, pool_mix_w,
        pool_scale, w_pool_o, w_out, norm_ffn_w, w_query, sub_keys, expert_u, expert_v,
        final_norm_w,
    )
    return second_block(
        x, positions_2, attn_norm_g_2, mlp_norm_g_2, diff_w_in_2, diff_w_out_2, diff_lam_q1_2,
        diff_lam_k1_2, diff_lam_q2_2, diff_lam_k2_2, diff_subln_g_2, moba_w_in_2, moba_w_out_2,
        swa_w_in_2, swa_b_in_2, swa_sinks_2, swa_w_out_2, mlp_w_up_2, mlp_w_down_2,
        final_norm_g_2,
    )


_drawn_inputs = setup_inputs


def setup_inputs(seed=0):
    import zlib

    import numpy as np

    out = dict(_drawn_inputs(seed))
    spreads = {}
    factors = {'q_norm_w': 8.0,
     'k_norm_w': 8.0,
     'pool_scale': 2.972,
     'mlp_norm_g_2': 3.204,
     'diff_lam_q2_2': 4.059,
     'diff_subln_g_2': 3.852,
     'swa_b_in_2': 25.668,
     'swa_sinks_2': 18.377,
     'final_norm_g_2': 7.86}
    for name, (base, spread) in spreads.items():
        noise = np.random.default_rng([zlib.crc32(name.encode()), seed]).standard_normal(out[name].shape)
        drawn = base * np.exp(spread * noise) if base else spread * noise
        out[name] = __import__('jax').numpy.asarray(drawn.astype(out[name].dtype))
    for name, factor in factors.items():
        out[name] = (out[name] * factor).astype(out[name].dtype)
    return out
```

```python
from contextlib import ExitStack

import concourse.bass as bass
import numpy as np
from concourse import mybir

F32 = mybir.dt.float32
I32 = mybir.dt.int32
U32 = mybir.dt.uint32
ALU = mybir.AluOpType
ACT = mybir.ActivationFunctionType
AX = mybir.AxisListType.X

P = 128
D = 1024
S = 256
NT = S // P
KC = D // P
UC = 512
RING = 4
DEPTH = 2
EPS = 1e-6
N_ADA = 6
HD1 = 128
NQ1, NKV1 = 8, 2
NPG = 4
PH = 8
NKEY = 128
NEXP = NKEY * NKEY
TOPK = 16
GB = 8
DB = 4
V0 = GB + 2 * NT * TOPK
LANDED = 16 * PH * NT * TOPK // GB
DEPTH2 = 4
HD2 = 64
ROT = 16
D_FF = 4096
SWA_IN = 1280
NSWA = 4
POOL_WINDOWS = (2, 4, 8, 16)

CONSTS = [("ident", 128), ("cos", 128), ("sin", 128), ("zero", 512), ("causal", 512),
          ("band", 512), ("pool", 2048), ("inv", 8), ("iota", 16)]
COFF = {}
CW = 0
for _n, _w in CONSTS:
    COFF[_n] = (CW, CW + _w)
    CW += _w


def const_table():
    t = np.zeros((P, CW), np.float32)

    def put(name, a):
        lo, hi = COFF[name]
        t[:, lo:hi] = a.reshape(P, hi - lo)

    put("ident", np.eye(P, dtype=np.float32))
    tok = np.arange(S)
    inv1 = (1.0 / (np.float32(10000.0) ** (np.arange(0, 64, 2, dtype=np.float32) / np.float32(64)))).astype(np.float32)
    ang = np.stack([(tok // 64).astype(np.float32)[:, None] * inv1,
                    (tok % 64).astype(np.float32)[:, None] * inv1], 1)
    for name, f in (("cos", np.cos), ("sin", np.sin)):
        a = f(ang.astype(np.float64)).astype(np.float32).reshape(NT, P, 64)
        put(name, a.transpose(1, 0, 2))
    q, k = tok[:, None], tok[None, :]
    for name, ok in (("causal", k <= q), ("band", (k <= q) & (q - k < 128))):
        m = np.where(ok, 0.0, -1e30).astype(np.float32).reshape(NT, P, S)
        put(name, m.transpose(1, 0, 2))
    pools = []
    for w in POOL_WINDOWS:
        lo = np.clip(tok - w // 2, 0, S)
        hi = np.clip(tok + w // 2, 0, S)
        m = ((k >= lo[:, None]) & (k < hi[:, None])) / (hi - lo)[:, None].astype(np.float64) - np.eye(S)
        pools.append(m.T.reshape(NT, P, S))
    put("pool", np.stack(pools).astype(np.float32).transpose(2, 0, 1, 3))
    put("inv", np.broadcast_to((np.float32(500000.0) ** (-np.arange(0, ROT, 2, dtype=np.float32) / np.float32(ROT))).astype(np.float32), (P, 8)))
    put("iota", np.broadcast_to(np.arange(16, dtype=np.float32), (P, 16)))
    return t


class Mixer:
    def __init__(self, nsub, join, width, vcol, kshare, vshare, nblk, scale, mask):
        self.nsub, self.join, self.width, self.vcol = nsub, join, width, vcol
        self.kshare, self.vshare, self.nblk, self.scale, self.mask = kshare, vshare, nblk, scale, mask
        self.nout = nsub // join

    def score_operands(self, s):
        if self.nsub == 8:
            return s, 8 + s // self.kshare, 0, 128
        c = s % 2
        return s // 2, 8 + s // self.kshare, 64 * c, 64 * c + 64

    def head_at(self, i, lag):
        d = i - self.join - lag
        return d // self.join if d >= 0 and d % self.join == 0 and d // self.join < self.nout else None

    def v_at(self, o):
        c = self.vcol + self.width * (o // self.vshare)
        return c, c + self.width


GQA = Mixer(8, 1, 128, 1280, 4, 4, 10, 128.0 ** -0.5, "zero")
DIFF = Mixer(16, 2, 128, 2048, 2, 1, 16, 0.125, "causal")
MOBA = Mixer(16, 1, 64, 2048, 2, 1, 16, 0.125, "causal")
SWA = Mixer(16, 1, 64, 1152, 8, 8, 10, 0.125, "band")
MIXERS2 = [DIFF, MOBA, SWA, DIFF]
LAM_INIT = [0.8 - 0.6 * float(np.exp(-0.3 * i)) for i in range(DEPTH2)]


class Counts:

    def __init__(self):
        self.unit = 0
        self.lin = 0
        self.tr = 0
        self.norm = 0
        self.xn = 0
        self.x = 0
        self.sc = 0
        self.out = 0
        self.slot = [0] * RING

    def next_slot(self):
        s = self.unit % RING
        self.unit += 1
        self.slot[s] += 1
        return s, 16 * self.slot[s]


INS1 = ["x", "c", "ada_w", "ada_b", "norm_mix_w", "w_in", "q_norm_w", "k_norm_w", "w_attn_o",
        "pool_mix_w", "pool_scale", "w_pool_o", "w_out", "norm_ffn_w", "w_query", "sub_keys",
        "expert_u", "expert_v", "final_norm_w"]
INS2 = ["positions_2", "attn_norm_g_2", "mlp_norm_g_2", "diff_w_in_2", "diff_w_out_2",
        "diff_lam_q1_2", "diff_lam_k1_2", "diff_lam_q2_2", "diff_lam_k2_2", "diff_subln_g_2",
        "moba_w_in_2", "moba_w_out_2", "swa_w_in_2", "swa_b_in_2", "swa_sinks_2", "swa_w_out_2",
        "mlp_w_up_2", "mlp_w_down_2", "final_norm_g_2"]


def program(nc, T, out):
    with ExitStack() as ctx:
        def sb(name, shape, dt=F32):
            return ctx.enter_context(nc.sbuf_tensor(name, shape, dt))

        def sem(name):
            return ctx.enter_context(nc.semaphore(name))

        ctx.enter_context(nc.allow_non_contiguous_dma(reason="small parameter vectors"))
        const = sb("const", [P, CW])

        def cst(name):
            lo, hi = COFF[name]
            return const[:, lo:hi]

        ident = cst("ident")
        x = sb("x_res", [P, NT, D])
        xn = sb("xn", [P, NT, D])
        xT = sb("xT", [P, KC, S])
        tokb = sb("tokb", [P, NT, D])
        proj = sb("proj", [P, NT, 4096])
        ring = sb("ring", [P, RING, KC, UC])
        vbuf = sb("vbuf", [P, GB, D])
        rowb = sb("rowb", [P, 2, D])
        prow = sb("prow", [P, P])
        pcol = sb("pcol", [P, P])
        modc = sb("modc", [P, 48])
        cact = sb("cact", [P, KC])
        aff = sb("aff", [P, 4, KC])
        wrow = sb("wrow", [P, 4, P])
        st = sb("st", [P, 64])
        sm = sb("sm", [P, 2, NT, S])
        pr = sb("pr", [P, 2, NT, S])
        pT = sb("pT", [P, 2, NT, S])
        rope_t = sb("rope_t", [P, 4, 256])
        cs2 = sb("cs2", [P, 2, NT, 8])
        ang = sb("ang", [P, 6, NT, 8])
        posi = sb("posi", [P, NT], I32)
        posf = sb("posf", [P, NT])
        sinks = sb("sinks", [P, 16])
        lamv = sb("lamv", [P, 4, HD2])
        vals = sb("vals", [P, 2, TOPK])
        idxu = sb("idxu", [P, 2, TOPK], U32)
        idxf = sb("idxf", [P, 2, TOPK])
        posu = sb("posu", [P, 3, TOPK], U32)
        posfl = sb("posfl", [P, 4, TOPK])
        base_f = sb("base_f", [P, 1])
        tops = sb("tops", [P, 4, TOPK])
        nmx = sb("nmx", [P, 4, 1])
        eidx = sb("eidx", [P, 4, TOPK], U32)
        hdot = sb("hdot", [P, 4, TOPK])
        gel = sb("gel", [P, 4, TOPK])
        eg = sb("eg", [P, 4, TOPK])
        ers = sb("ers", [P, 4, 2])
        actw = sb("actw", [P, 4, TOPK])

        lin = ctx.enter_context(nc.psum_tensor("lin", [P, 4, 512], F32))
        psT = ctx.enter_context(nc.psum_tensor("psT", [P, 2, 512], F32))
        psS = ctx.enter_context(nc.psum_tensor("psS", [P, 2, 512], F32))

        ubuf = proj[:, :, :].rearrange("p t (b d) -> p (t b) d", d=D)
        poolw = vbuf[:, 0:4, :]
        qkT = vbuf[:, 4:8, :].rearrange("p b (h s) -> p (b h) s", s=S)
        mT = pT[:, :, :, :].rearrange("p a b s -> p (a b) s")
        mixT = pr[:, :, :, :].rearrange("p a b s -> p (a b) s")
        qTx = sm[:, :, :, :].rearrange("p a b s -> p (a b) s")
        skT = pT[:, 0, :, :].rearrange("p a (b k) -> p (a b) k", k=NKEY)
        topb = rope_t[:, :, :].rearrange("p a (b n) -> p a b n", b=2)
        skn = ring[:, 2, 0:2, :].rearrange("p j (q d) -> p j q d", q=2)
        diag = ring[:, 3, 0, :].rearrange("p (b n) -> p b n", b=DB)
        mixw = vbuf[:, 7, 512:1024].rearrange("p (g n) -> p g n", g=NPG)
        ones = vbuf[:, 7, 0:P]
        ada_acc = proj[:, 0, 0:2 * UC].rearrange("p (a n) -> p a n", a=2)
        sc2 = xn[:, :, :].rearrange("p t (b n) -> p (t b) n", n=256)
        bias_row = vbuf[:, 0:2, :].rearrange("p a d -> p (a d)")
        aT = proj[:, 0, :].rearrange("p (b f s) -> p b f s", b=4, s=S)

        s_const = sem("const_loaded")
        s_par = sem("params_loaded")
        s_poolw = sem("pool_weights_loaded")
        ld = [sem(f"ring_slot_loaded{i}") for i in range(RING)]
        x_ready = sem("x_ready")
        n_sq = sem("norm_squares")
        n_rec = sem("norm_reciprocal")
        n_rstd = sem("norm_rstd")
        xn_ready = sem("xn_ready")
        tr_done = sem("transposed")
        tr_used = sem("transposes_copied")
        lin_done = sem("linear_done")
        lin_used = sem("linear_copied")
        p_tr = sem("params_transposed")
        p_col = sem("params_in_columns")
        s_cact = sem("c_activated")
        s_ada = sem("ada_done")
        s_mod = sem("mod_ready")
        acc_ready = sem("ada_partial_sums_ready")
        s_gbc = sem("gate_rows_copied")
        qk_ready = sem("qk_ready")
        hn_sq = sem("head_norm_mean_ready")
        hn_rs = sem("head_norm_rstd_ready")
        sc_done = sem("scores_done")
        sc_used = sem("scores_copied")
        sm_max = sem("score_max_ready")
        ex_done = sem("exp_done")
        pn_done = sem("probs_ready")
        pt_copied = sem("probs_transposed_copied")
        pt_done = sem("probs_transposed")
        pv_done = sem("heads_done")
        pv_used = sem("heads_copied")
        pl_mm = sem("pool_matmuls")
        pl_cp = sem("pool_copied")
        tok_ready = sem("attention_rows_ready")
        merged_ready = sem("merged_ready")
        xf_ready = sem("xf_rows_ready")
        sk_ld = [sem(f"sub_keys_loaded{i}") for i in range(2)]
        sk_done = sem("sub_keys_transposed")
        sk_used = sem("sub_keys_copied")
        q_done = sem("peer_query_done")
        q_used = sem("peer_query_copied")
        ps_done = sem("peer_scores_done")
        ps_used = sem("peer_scores_copied")
        idx_ready = sem("expert_indices_ready")
        u_ld = [sem(f"u_rows_landed{i}") for i in range(GB)]
        v_ld = [sem(f"v_rows_landed{i}") for i in range(GB)]
        u_free = sem("u_buffer_free")
        v_free = sem("v_buffer_free")
        h_ready = sem("expert_dots_ready")
        gate_ready = sem("router_exp_ready")
        gelu_ready = sem("gelu_ready")
        w_ready = sem("expert_weights_ready")
        dg_done = sem("diag_ready")
        y_open = sem("y_opened")
        up_done = sem("mlp_up_done")
        rl_done = sem("relu_done")
        a_done = sem("mlp_act_ready")
        a_free = sem("mlp_act_buffer_free")
        lam_e = sem("lambda_exponents")
        lam_x = sem("lambda_exps")
        rope_arg = sem("rope_args_ready")
        rope_cs = sem("rope_tables_ready")
        dchain = sem("dve_step")
        achain = sem("act_step")
        pchain = sem("pool_step")
        s_out = sem("output_stored")
        arrive = sem("layer_arrived")
        go = sem("layer_go")
        waits_met = sem("waits_met")
        cleared = [ld, sk_ld, [s_par, s_poolw, x_ready, n_sq, n_rec, n_rstd,
                   xn_ready, tr_done, tr_used, lin_done, lin_used, p_tr, p_col, s_cact, s_ada,
                   s_mod, acc_ready, s_gbc, qk_ready, hn_sq, hn_rs, sc_done, sc_used, sm_max,
                   ex_done, pn_done, pt_copied, pt_done, pv_done, pv_used, pl_mm, pl_cp, tok_ready,
                   merged_ready, xf_ready, sk_done, sk_used, q_done, q_used, ps_done, ps_used,
                   idx_ready, u_free, v_free, h_ready, gate_ready, gelu_ready, w_ready, 
                   dg_done, y_open, up_done, rl_done, a_done, a_free, dchain, achain]]

        def wait_loop(eng, s, value, alone=False):
            eng.wait_ge(s, value)
            if alone and not isinstance(value, int):
                eng.sem_inc(waits_met, 1)

        def layer_end(eng, l):
            eng.sem_inc(arrive, 1)
            wait_loop(eng, go, l + 1)

        block = ctx.enter_context(nc.Block())

        @block.sync
        def _(sp):
            sp.dma_start(const[:, :], T["consts"]).then_inc(s_const, 16)
            sp.dma_start(x[:, :, :], T["x"][0].rearrange("(t p) d -> p t d", p=P)).then_inc(s_const, 16)

            used = []

            def unit(C, src, used_up, kc=KC, cols=UC):
                n = C.unit
                slot, _ = C.next_slot()
                if n >= RING:
                    sp.wait_ge(*used[n - RING])
                used.append(used_up)
                dst = ring[:, slot, :, :].rearrange("p k n -> p (k n)")[:, 0:kc * cols]
                sp.dma_start(dst.rearrange("p (k n) -> p k n", k=kc), src).then_inc(ld[slot], 16)

            def cols_of(w, lo, n):
                return w.rearrange("(k p) n -> p k n", p=P)[:, :, lo:lo + n]

            with sp.Fori(0, DEPTH) as l:
                C = Counts()
                used.clear()
                sp.dma_start(prow[0:48, :], T["ada_b"][l].rearrange("(r j) -> r j", j=P)).then_inc(s_par, 16)
                sp.dma_start(prow[48:56, :], T["norm_mix_w"][l].rearrange("(r j) -> r j", j=P)).then_inc(s_par, 16)
                sp.dma_start(prow[56:64, :], T["norm_ffn_w"][l].rearrange("(r j) -> r j", j=P)).then_inc(s_par, 16)
                sp.dma_start(prow[64:72, :], T["c"].rearrange("a (r j) -> (a r) j", j=P)).then_inc(s_par, 16)
                sp.dma_start(prow[72:76, :], T["pool_scale"][l].rearrange("(r j) -> r j", j=P)).then_inc(s_par, 16)
                sp.dma_start(wrow[:, 0, :], T["q_norm_w"][l].rearrange("(a d) -> a d", a=1).to_broadcast([P, HD1])).then_inc(s_par, 16)
                sp.dma_start(wrow[:, 1, :], T["k_norm_w"][l].rearrange("(a d) -> a d", a=1).to_broadcast([P, HD1])).then_inc(s_par, 16)
                sp.dma_start(mixw[:, :, :], T["pool_mix_w"][l].rearrange("g c d -> c g d")).then_inc(s_par, 16)
                for g in range(2):
                    lo = (3 * g + 2) * D
                    sp.dma_start(rowb[:, g, :], T["ada_b"][l][lo:lo + D].rearrange("(a d) -> a d", a=1).to_broadcast([P, D])).then_inc(s_par, 16)
                for n in range(N_ADA * D // UC):
                    unit(C, cols_of(T["ada_w"][l], n * UC, UC), (acc_ready, n + 1))
                sp.dma_start(poolw, T["w_pool_o"][l].rearrange("(k p) n -> p k n", p=P)).then_inc(s_poolw, 16)
                for n in range(8):
                    unit(C, cols_of(T["w_in"][l], n * UC, UC), (lin_done, n + 1))
                for n in range(2):
                    unit(C, cols_of(T["w_attn_o"][l], n * UC, UC), (lin_done, n + 9))
                for n in range(2):
                    unit(C, cols_of(T["w_out"][l], n * UC, UC), (lin_done, n + 13))
                def head_loads(h, j, first):
                    if first:
                        sp.wait_ge(lin_done, 14)
                    else:
                        wait_loop(sp, q_done, h - 1)
                    sp.dma_start(ring[:, j, :, :], cols_of(T["w_query"][l], h * UC, UC)
                                 if isinstance(h, int) else
                                 T["w_query"][l].rearrange("(k p) (h n) -> h p k n", p=P, n=UC)[h]).then_inc(ld[j], 16)
                    if not first:
                        wait_loop(sp, sk_done, h - 1)
                    sp.dma_start(skn[:, j, :, :], T["sub_keys"][l].rearrange("h q n d -> h n q d")[h]).then_inc(sk_ld[j], 16)

                head_loads(0, 0, True)
                head_loads(1, 1, True)
                with sp.Fori(1, PH // 2) as hp:
                    for j in range(2):
                        head_loads(2 * hp + j, j, False)
                sp.wait_ge(x_ready, 2)
                wait_loop(sp, arrive, 4 * l + 4, alone=True)
                for group in cleared:
                    for s in group:
                        sp.sem_clear(s)
                sp.sem_inc(go, 1)

            C = Counts()
            used.clear()
            sp.dma_start(rowb[:, 0, :], T["final_norm_w"].rearrange("(a d) -> a d", a=1).to_broadcast([P, D])).then_inc(s_par, 16)
            sp.dma_start(rowb[:, 1, :], T["final_norm_g_2"].rearrange("(a d) -> a d", a=1).to_broadcast([P, D])).then_inc(s_par, 16)
            sp.dma_start(prow[0:32, :], T["attn_norm_g_2"].rearrange("l (r j) -> (l r) j", j=P)).then_inc(s_par, 16)
            sp.dma_start(prow[32:64, :], T["mlp_norm_g_2"].rearrange("l (r j) -> (l r) j", j=P)).then_inc(s_par, 16)
            sp.dma_start(posi[:, :], T["positions_2"].rearrange("a (t p) -> p (a t)", p=P)).then_inc(s_par, 16)
            sp.dma_start(wrow[:, 0:2, :], T["diff_subln_g_2"].rearrange("(a l) d -> a l d", a=1).to_broadcast([P, 2, P])).then_inc(s_par, 16)
            sp.dma_start(sinks[:, :], T["swa_sinks_2"].to_broadcast([P, 16])).then_inc(s_par, 16)
            sp.dma_start(bias_row[:, 0:SWA_IN], T["swa_b_in_2"].to_broadcast([P, SWA_IN])).then_inc(s_par, 16)
            for i, m in enumerate(MIXERS2):
                slot = i // 3
                if m is DIFF:
                    if slot:
                        sp.wait_ge(lam_x, 1)
                    for v, name in enumerate(("q1", "k1", "q2", "k2")):
                        sp.dma_start(lamv[:, v, :], T[f"diff_lam_{name}_2"][slot:slot + 1, :].to_broadcast([P, HD2])).then_inc(lam_e, 16)
                w_in, w_o, n_in, cols = {0: (T["diff_w_in_2"], T["diff_w_out_2"], 6, UC),
                                         1: (T["moba_w_in_2"], T["moba_w_out_2"], 6, UC),
                                         2: (T["swa_w_in_2"], T["swa_w_out_2"], NSWA, SWA_IN // NSWA)}[i % 3]
                for n in range(n_in):
                    C.lin += 1
                    unit(C, cols_of(w_in[slot], n * cols, cols), (lin_done, C.lin), cols=cols)
                for n in range(2):
                    C.lin += 1
                    unit(C, cols_of(w_o[slot], n * UC, UC), (lin_done, C.lin))
                C.lin += 2
                ub = 8 * i
                up = T["mlp_w_up_2"][i].rearrange("(k p) (f n) -> f p k n", p=P, n=UC)
                down = T["mlp_w_down_2"][i].rearrange("(f k p) n -> f p k n", p=P, k=4)

                def up_load(n):
                    unit(C, up[n], (up_done, ub + n + 1))

                def down_load(n):
                    unit(C, down[n], (a_free, ub + n + 3), kc=4, cols=D)

                up_load(0)
                up_load(1)
                down_load(0)
                u0 = C.unit
                slots = [(u0 + k) % RING for k in range(4)]
                with sp.Fori(0, 3) as r:
                    for k, src in enumerate((up[2 * r + 2], down[2 * r + 1], up[2 * r + 3], down[2 * r + 2])):
                        if k % 2 == 0:
                            wait_loop(sp, up_done, 2 * r + (ub + 1 + k // 2))
                        else:
                            wait_loop(sp, a_free, 2 * r + (ub + 2 + k // 2))
                        dst = ring[:, slots[k], :, :].rearrange("p k n -> p (k n)")
                        kc = KC if k % 2 == 0 else 4
                        sp.dma_start(dst.rearrange("p (k n) -> p k n", k=kc), src).then_inc(ld[slots[k]], 16)
                for _ in range(12):
                    C.next_slot()
                used += [None] * 8 + [(up_done, ub + 7), (a_free, ub + 8), (up_done, ub + 8), (a_free, ub + 9)]
                down_load(7)
            sp.wait_ge(xn_ready, 4 * 2 * DEPTH2 // 2 + 2)
            sp.dma_start(out[0].rearrange("(t p) d -> p t d", p=P), xn[:, :, :]).then_inc(s_out, 16)
            sp.wait_ge(s_out, 16)

        @block.tensor
        def _(pe):
            def tr_group(C, srcs):
                if C.tr >= 2:
                    pe.wait_ge(tr_used, C.tr - 1)
                for n, src in enumerate(srcs):
                    mm = pe.transpose(psT[:, C.tr % 2, n * P:(n + 1) * P], src, ident)
                mm.then_inc(tr_done, 1)
                C.tr += 1

            def tr_all(C, buf):
                for k in range(0, KC, 2):
                    tr_group(C, [buf[:, t, (k + b) * P:(k + b + 1) * P] for b in range(2) for t in range(NT)])

            def norm(C):
                C.norm += 1
                C.xn += 2
                pe.wait_ge(xn_ready, C.xn)
                tr_all(C, xn)

            def linear(C, lhs, kc, rhs, cols):
                pair = 2 * (C.lin % 2)
                if C.lin >= 2:
                    pe.wait_ge(lin_used, C.lin - 1)
                for t in range(NT):
                    for k in range(kc):
                        mm = pe.matmul(lin[:, pair + t, 0:cols], lhs[:, k, t * P:(t + 1) * P], rhs[:, k, :],
                                       start=(k == 0), stop=(k == kc - 1))
                C.lin += 1
                return mm.then_inc(lin_done, 1)

            def linear_units(C, lhs, n, cols=UC):
                for _ in range(n):
                    slot, landed = C.next_slot()
                    pe.wait_ge(ld[slot], landed)
                    w = ring[:, slot, :, :].rearrange("p k n -> p (k n)")[:, 0:KC * cols].rearrange("p (k n) -> p k n", k=KC)
                    linear(C, lhs, KC, w, cols)

            def attention(C, m):
                pe.wait_ge(lin_used, C.lin)
                tr0 = C.tr
                if C.tr:
                    pe.wait_ge(tr_used, C.tr)
                for b in range(0, m.nblk, 2):
                    srcs = []
                    for blk in (b, b + 1):
                        for t in range(NT):
                            if m is SWA and blk >= 8:
                                srcs.append(xn[:, t, (blk - 8) * P:(blk - 7) * P])
                            else:
                                srcs.append(proj[:, t, blk * P:(blk + 1) * P])
                    tr_group(C, srcs)
                pe.wait_ge(tr_used, C.tr)
                for i in range(m.nsub + 3):
                    if i < m.nsub:
                        g = C.sc + i
                        qb, kb, lo, hi = m.score_operands(i)
                        if g >= 2:
                            pe.wait_ge(sc_used, g - 1)
                        for t in range(NT):
                            mm = pe.matmul(psS[:, g % 2, t * S:(t + 1) * S], qkT[lo:hi, qb, t * P:(t + 1) * P],
                                           qkT[lo:hi, kb, :], start=True, stop=True)
                        mm.then_inc(sc_done, 1)
                    o = m.head_at(i, 1)
                    if o is not None:
                        g = C.out + o
                        pe.wait_ge(pn_done, g + 1)
                        if g >= 2:
                            pe.wait_ge(pt_copied, g - 1)
                        for kt in range(NT):
                            for t in range(NT):
                                mm = pe.transpose(psT[:, g % 2, kt * S + t * P:kt * S + (t + 1) * P],
                                                  pr[:, g % 2, t, kt * P:(kt + 1) * P], ident)
                        mm.then_inc(pt_done, 1)
                    o = m.head_at(i, 2)
                    if o is not None:
                        values(C, m, o)
                C.sc += m.nsub
                C.out += m.nout

            def values(C, m, o):
                g = C.out + o
                pe.wait_ge(pt_copied, g + 1)
                if g >= 2:
                    pe.wait_ge(pv_used, g - 1)
                a, b = m.v_at(o)
                for t in range(NT):
                    for kt in range(NT):
                        mm = pe.matmul(lin[:, g % 2, t * m.width:(t + 1) * m.width],
                                       pT[:, g % 2, kt, t * P:(t + 1) * P], proj[:, kt, a:b],
                                       start=(kt == 0), stop=(kt == NT - 1))
                mm.then_inc(pv_done, 1)

            pe.wait_ge(s_const, 32)
            with pe.Fori(0, DEPTH) as l:
                C = Counts()
                pe.wait_ge(s_par, 160)
                pe.transpose(psT[:, 0, 0:76], prow[0:76, :], ident[0:76, 0:76]).then_inc(p_tr, 1)
                for n in range(N_ADA * D // UC):
                    C.next_slot()
                    pe.wait_ge(acc_ready, n + 1)
                    acc = ada_acc[:, n % 2, :]
                    if n // 2 % 3 == 2:
                        mm = pe.matmul(lin[:, 2 * (n // 6) + n % 2, :], ones, acc, start=True, stop=True)
                    else:
                        for j in range(4):
                            mm = pe.matmul(psS[:, 0, 4 * n + j:4 * n + j + 1], acc[:, j * P:(j + 1) * P], ones[:, 0:1],
                                           start=True, stop=True)
                    mm.then_inc(s_ada, 1)
                pe.wait_ge(s_gbc, 1)
                C.tr = 0
                norm(C)
                pe.wait_ge(tr_used, C.tr)
                for n in range(8):
                    slot, landed = C.next_slot()
                    pe.wait_ge(ld[slot], landed)
                    linear(C, xT, KC, ring[:, slot, :, :], UC)
                pe.wait_ge(qk_ready, 1)
                attention(C, GQA)
                pe.wait_ge(pt_copied, C.out)
                pe.wait_ge(pv_used, C.out)
                for g in range(NPG):
                    for kt in range(NT):
                        lo = COFF["pool"][0] + (g * NT + kt) * S
                        mm = pe.matmul(psS[:, g // 2, (g % 2) * S:(g % 2 + 1) * S],
                                       proj[:, kt, 1536 + g * P:1536 + (g + 1) * P], const[:, lo:lo + S],
                                       start=(kt == 0), stop=(kt == NT - 1))
                mm.then_inc(pl_mm, 1)
                pe.wait_ge(pl_cp, 1)
                for g in range(NPG):
                    mm = pe.matmul(psS[:, g // 2, (g % 2) * S:(g % 2 + 1) * S], mixw[:, g, :], mT[:, g, :],
                                   start=True, stop=True)
                mm.then_inc(pl_mm, 1)
                pe.wait_ge(tok_ready, 1)
                tr_all(C, tokb)
                pe.wait_ge(tr_used, C.tr)
                for n in range(2):
                    slot, landed = C.next_slot()
                    pe.wait_ge(ld[slot], landed)
                    linear(C, xT, KC, ring[:, slot, :, :], UC)
                pe.wait_ge(pl_cp, 2)
                pe.wait_ge(s_poolw, 16)
                for n in range(2):
                    linear(C, mixT, 4, poolw[:, :, n * UC:(n + 1) * UC], UC)
                pe.wait_ge(merged_ready, 1)
                tr_all(C, xn)
                pe.wait_ge(tr_used, C.tr)
                for n in range(2):
                    slot, landed = C.next_slot()
                    pe.wait_ge(ld[slot], landed)
                    linear(C, xT, KC, ring[:, slot, :, :], UC)
                norm(C)
                pe.wait_ge(tr_used, C.tr)
                for t in range(NT):
                    for k in range(0, KC, 4):
                        tr_group(C, [xT[:, k + b, t * P:(t + 1) * P] for b in range(4)])
                pe.wait_ge(tr_used, C.tr)
                pe.wait_ge(lin_used, C.lin)

                for b in range(4):
                    mm = pe.matmul(lin[:, b, :], ident, cst("zero"), start=True, stop=False, skip_group_check=True)
                pe.sem_inc(v_free, V0)
                qbase = C.slot[0]

                def query(h, j, first):
                    wait_loop(pe, sk_ld[j], 16 * (1 if first else 1) if isinstance(h, int) and h < 2 else (h - j) * 8 + 16)
                    if not (isinstance(h, int) and h == 0):
                        wait_loop(pe, ps_used, h)
                        wait_loop(pe, q_used, h)
                        wait_loop(pe, sk_used, h)
                    for q in range(2):
                        for c in range(2):
                            mm = pe.transpose(psS[:, 0, (2 * q + c) * NKEY:(2 * q + c + 1) * NKEY],
                                              skn[:, j, q, c * P:(c + 1) * P], ident)
                    mm.then_inc(sk_done, 1)
                    wait_loop(pe, ld[j], (h - j) * 8 + 16 * (qbase + 1))
                    for b in range(4):
                        for k in range(KC):
                            mm = pe.matmul(psT[:, b // 2, (b % 2) * S:(b % 2 + 1) * S], ring[:, j, k, b * P:(b + 1) * P],
                                           xT[:, k, :], start=(k == 0), stop=(k == KC - 1))
                    mm.then_inc(q_done, 1)
                    wait_loop(pe, q_used, h + 1)
                    wait_loop(pe, sk_used, h + 1)
                    for t in range(NT):
                        for q in range(2):
                            for c in range(2):
                                mm = pe.matmul(psS[:, 1, (2 * t + q) * NKEY:(2 * t + q + 1) * NKEY],
                                               qTx[:, 2 * q + c, t * P:(t + 1) * P], skT[:, 2 * q + c, :],
                                               start=(c == 0), stop=(c == 1))
                    mm.then_inc(ps_done, 1)

                def expert_sum(h, j, t):
                    for k in range(TOPK):
                        n = 16 * (NT * j + t) + k
                        wait_loop(pe, dg_done, (h - j) * 32 + n + 1)
                        wait_loop(pe, v_ld[n % GB], l * LANDED + (h - j) * 64 + 16 * (n // GB + 1))
                        for half in range(2):
                            mm = pe.matmul(lin[:, 2 * half + t, :], diag[:, n % DB, :],
                                           vbuf[:, n % GB, half * 512:(half + 1) * 512], start=False, stop=False,
                                           skip_group_check=True)
                        mm.then_inc(v_free, 1)

                query(0, 0, True)
                with pe.Fori(0, PH // 2 - 1) as hp:
                    query(2 * hp + 1, 1, False)
                    for t in range(NT):
                        expert_sum(2 * hp, 0, t)
                    query(2 * hp + 2, 0, False)
                    for t in range(NT):
                        expert_sum(2 * hp + 1, 1, t)
                query(PH - 1, 1, False)
                for j in range(2):
                    for t in range(NT):
                        expert_sum(PH - 2 + j, j, t)
                for b in range(4):
                    mm = pe.matmul(lin[:, b, :], ident, cst("zero"), start=False, stop=True, skip_group_check=True)
                mm.then_inc(lin_done, 2)
                C.lin += 2
                layer_end(pe, l)

            C = Counts()
            pe.wait_ge(s_par, 128)
            pe.transpose(psT[:, 0, 0:64], prow[0:64, :], ident[0:64, 0:64]).then_inc(p_tr, 1)
            pe.wait_ge(p_col, 1)
            for i, m in enumerate(MIXERS2):
                norm(C)
                pe.wait_ge(tr_used, C.tr)
                n_in, cols = (NSWA, SWA_IN // NSWA) if m is SWA else (6, UC)
                for n in range(n_in):
                    slot, landed = C.next_slot()
                    pe.wait_ge(ld[slot], landed)
                    w = ring[:, slot, :, :].rearrange("p k n -> p (k n)")[:, 0:KC * cols].rearrange("p (k n) -> p k n", k=KC)
                    linear(C, xT, KC, w, cols)
                pe.wait_ge(qk_ready, i + 1)
                attention(C, m)
                pe.wait_ge(pt_copied, C.out)
                pe.wait_ge(pv_used, C.out)
                pe.wait_ge(tok_ready, i + 1)
                tr_all(C, tokb)
                pe.wait_ge(tr_used, C.tr)
                for n in range(2):
                    slot, landed = C.next_slot()
                    pe.wait_ge(ld[slot], landed)
                    linear(C, xT, KC, ring[:, slot, :, :], UC)
                norm(C)
                pe.wait_ge(tr_used, C.tr)
                pe.wait_ge(lin_used, C.lin)
                if i == 0:
                    pe.sem_inc(a_free, 2)
                ub = i * 8

                def bank(n):
                    return (psT, psS)[n % 2]

                def up(n, b, slot, landed):
                    wait_loop(pe, ld[slot], landed)
                    if not (isinstance(n, int) and n + ub < 2):
                        wait_loop(pe, rl_done, n + ub - 1)
                    for f in range(4):
                        for k in range(KC):
                            mm = pe.matmul(bank(b)[:, f // 2, (f % 2) * S:(f % 2 + 1) * S],
                                           ring[:, slot, k, f * P:(f + 1) * P], xT[:, k, :],
                                           start=(k == 0), stop=(k == KC - 1))
                    mm.then_inc(up_done, 1)

                def down(n, b, slot, landed, first=False, last=False):
                    wait_loop(pe, ld[slot], landed)
                    wait_loop(pe, a_done, n + ub + 1)
                    w = ring[:, slot, :, :].rearrange("p k n -> p (k n)").rearrange("p (k n) -> p k n", k=4)
                    for t in range(NT):
                        for half in range(2):
                            for k in range(4):
                                mm = pe.matmul(lin[:, 2 * half + t, :], aT[:, b, k, t * P:(t + 1) * P],
                                               w[:, k, half * 512:(half + 1) * 512], start=(first and k == 0),
                                               stop=(last and k == 3), skip_group_check=True)
                    mm.then_inc(a_free, 1)
                    if last:
                        pe.wait_ge(a_free, ub + 10)
                        pe.sem_inc(lin_done, 2)

                up(0, 0, *C.next_slot())
                up(1, 1, *C.next_slot())
                down(0, 0, *C.next_slot(), first=True)
                u = [C.next_slot() for _ in range(4)]
                with pe.Fori(0, 3) as r:
                    up(2 * r + 2, 0, u[0][0], 16 * r + u[0][1])
                    down(2 * r + 1, 1, u[1][0], 16 * r + u[1][1])
                    up(2 * r + 3, 1, u[2][0], 16 * r + u[2][1])
                    down(2 * r + 2, 0, u[3][0], 16 * r + u[3][1])
                for _ in range(8):
                    C.next_slot()
                down(7, 1, *C.next_slot(), last=True)
                C.lin += 2

        @block.scalar
        def _(act):
            chain = [0]

            def link(ins):
                chain[0] += 1
                ins.then_inc(achain, 1)
                act.wait_ge(achain, chain[0])

            def norm(C):
                if C.x:
                    act.wait_ge(x_ready, C.x)
                n = C.norm
                for t in range(NT):
                    if t:
                        act.wait_ge(n_sq, 2 * n + 1)
                    elif n:
                        act.wait_ge(n_rstd, n)
                    act.activation(tokb[:, 0, :], x[:, t, :], ACT.Square, accum_out=st[:, t:t + 1]).then_inc(n_sq, 1)
                act.wait_ge(n_rec, n + 1)
                act.activation(st[:, 4:6], st[:, 2:4], ACT.Sqrt).then_inc(n_rstd, 1)
                C.norm += 1
                C.xn += 2

            def attention(C, m):
                for i in range(m.nsub + 2):
                    if i < m.nsub:
                        g = C.sc + i
                        act.wait_ge(sm_max, g + 1)
                        o = C.out + i // m.join
                        if m.join == 1:
                            if o >= 2:
                                act.wait_ge(pt_done, o - 1)
                        else:
                            if i >= 2:
                                act.wait_ge(pn_done, o)
                            if o >= 2 and i % 2 == 0:
                                act.wait_ge(pt_done, o - 1)
                        dst = pr if m.join == 1 else None
                        for t in range(NT):
                            if m.join == 1:
                                to = pr[:, g % 2, t, :]
                            else:
                                to = rope_t[:, 2 * (g % 2) + t, 0:S]
                            a = act.activation(to, sm[:, g % 2, t, :], ACT.Exp, bias=st[:, 12 + 2 * (g % 2) + t:13 + 2 * (g % 2) + t],
                                               accum_out=st[:, 16 + 2 * (g % 2) + t:17 + 2 * (g % 2) + t])
                        if m is SWA:
                            a = act.activation(st[:, 20 + 2 * (g % 2):22 + 2 * (g % 2)], st[:, 12 + 2 * (g % 2):14 + 2 * (g % 2)],
                                               ACT.Exp, bias=sinks[:, i:i + 1])
                        a.then_inc(ex_done, 1)
                    if m.head_at(i, 1) is not None:
                        g = C.out + m.head_at(i, 1)
                        act.wait_ge(pt_done, g + 1)
                        if g >= 2:
                            act.wait_ge(pv_done, g - 1)
                        act.activation(pT[:, g % 2, :, :].rearrange("p a s -> p (a s)"), psT[:, g % 2, :], ACT.Copy).then_inc(pt_copied, 1)
                C.sc += m.nsub
                C.out += m.nout

            act.wait_ge(s_const, 32)
            with act.Fori(0, DEPTH) as l:
                C = Counts()
                chain[0] = 0
                act.wait_ge(p_col, 1)
                act.activation(cact[:, :], pcol[:, 64:72], ACT.Silu).then_inc(s_cact, 1)
                norm(C)
                for n in range(8):
                    act.wait_ge(lin_done, C.lin + 1)
                    pair = 2 * (C.lin % 2)
                    a = act.activation(proj[:, :, n * UC:(n + 1) * UC], lin[:, pair:pair + 2, :],
                                       ACT.Copy if n < 4 else ACT.Sigmoid)
                    a.then_inc(lin_used, 1)
                    C.lin += 1
                    if n == 2:
                        act.wait_ge(hn_sq, 1)
                        act.activation(st[:, 44:64], st[:, 24:44], ACT.Sqrt).then_inc(hn_rs, 1)
                attention(C, GQA)
                act.wait_ge(pl_mm, 1)
                act.wait_ge(pv_done, C.out)
                act.activation(mT.rearrange("p a s -> p (a s)"), psS[:, :, :].rearrange("p b n -> p (b n)"), ACT.Copy).then_inc(pl_cp, 1)
                act.wait_ge(pl_mm, 2)
                act.wait_ge(pt_done, C.out)
                for g in range(NPG):
                    a = act.activation(mixT[:, g, :], psS[:, g // 2, (g % 2) * S:(g % 2 + 1) * S], ACT.Copy, scale=pcol[:, 72 + g:73 + g])
                a.then_inc(pl_cp, 1)
                C.x += 1
                act.wait_ge(tr_used, 4 + 5 + 4)
                norm(C)

                def query_copies(h):
                    if not (isinstance(h, int) and h == 0):
                        wait_loop(act, ps_done, h)
                    wait_loop(act, sk_done, h + 1)
                    act.activation(skT.rearrange("p a k -> p (a k)"), psS[:, 0, :], ACT.Copy).then_inc(sk_used, 1)
                    wait_loop(act, q_done, h + 1)
                    act.activation(qTx.rearrange("p a s -> p (a s)"), psT[:, :, :].rearrange("p b n -> p (b n)"), ACT.Copy).then_inc(q_used, 1)

                def expert_weights(h, j, t):
                    cb = NT * j + t
                    c = (h - j) * 2 + cb
                    wait_loop(act, idx_ready, c + 1)
                    act.activation(eg[:, cb, :], tops[:, cb, :], ACT.Exp, bias=nmx[:, cb, :],
                                   accum_out=ers[:, cb, 0:1]).then_inc(gate_ready, 1)
                    wait_loop(act, h_ready, c * 16 + 16)
                    act.activation(gel[:, cb, :], hdot[:, cb, :], ACT.Gelu).then_inc(gelu_ready, 1)
                    wait_loop(act, w_ready, c + 1)
                    for k in range(TOPK):
                        n = 16 * cb + k
                        wait_loop(act, v_free, (h - j) * 32 + (n + 1 - DB + V0))
                        act.activation(diag[:, n % DB, :], ident, ACT.Copy, scale=actw[:, cb, k:k + 1]).then_inc(dg_done, 1)

                query_copies(0)
                with act.Fori(0, PH // 2 - 1) as hp:
                    query_copies(2 * hp + 1)
                    for t in range(NT):
                        expert_weights(2 * hp, 0, t)
                    query_copies(2 * hp + 2)
                    for t in range(NT):
                        expert_weights(2 * hp + 1, 1, t)
                query_copies(PH - 1)
                for j in range(2):
                    for t in range(NT):
                        expert_weights(PH - 2 + j, j, t)
                layer_end(act, l)

            C = Counts()
            act.wait_ge(rope_arg, 1)
            act.activation(cs2[:, :, :, :].rearrange("p a t f -> p (a t f)"), ang[:, 4:6, :, :].rearrange("p a t f -> p (a t f)"), ACT.Sin).then_inc(rope_cs, 1)
            norm(C)
            C.x = 1
            for i, m in enumerate(MIXERS2):
                if m is DIFF:
                    act.wait_ge(lam_x, 3 * (i // 3) + 1)
                    act.activation(st[:, 8:10], st[:, 6:8], ACT.Exp).then_inc(lam_x, 1)
                norm(C)
                if m is SWA:
                    C.lin += NSWA
                else:
                    for n in range(6):
                        act.wait_ge(lin_done, C.lin + 1)
                        pair = 2 * (C.lin % 2)
                        act.activation(proj[:, :, n * UC:(n + 1) * UC], lin[:, pair:pair + 2, :], ACT.Copy).then_inc(lin_used, 1)
                        C.lin += 1
                attention(C, m)
                if m is DIFF:
                    act.wait_ge(hn_sq, i // 3 + 1)
                    act.activation(st[:, 44:60], st[:, 24:40], ACT.Sqrt).then_inc(hn_rs, 1)
                C.x += 1
                C.lin += 2
                norm(C)
                ub = i * 8

                def relu(n, b):
                    wait_loop(act, up_done, n + ub + 1)
                    wait_loop(act, a_done, n + ub - 1) if not (isinstance(n, int) and n + ub < 2) else None
                    src = (psT, psS)[b]
                    act.activation(rl(b), src[:, :, :].rearrange("p b n -> p (b n)"), ACT.Relu).then_inc(rl_done, 1)

                def rl(b):
                    return proj[:, 1, b * 1024:(b + 1) * 1024]

                for n in range(2):
                    relu(n, n)
                with act.Fori(1, 4) as r:
                    for b in range(2):
                        relu(2 * r + b, b)
                C.x += 1
                C.lin += 2
            norm(C)

        @block.vector
        def _(dve):
            chain = [0]

            def link(ins):
                chain[0] += 1
                ins.then_inc(dchain, 1)
                dve.wait_ge(dchain, chain[0])

            def restart_chain():
                dve.sem_clear(dchain)
                chain[0] = 0

            def norm(C, gain_row=None):
                n = C.norm
                dve.wait_ge(n_sq, 2 * n + 2)
                link(dve.tensor_scalar(st[:, 2:4], st[:, 0:2], 1.0 / D, EPS, ALU.mult, ALU.add))
                link(dve.reciprocal(st[:, 2:4], st[:, 2:4]))
                dve.sem_inc(n_rec, 1)
                dve.wait_ge(n_rstd, n + 1)
                for t in range(NT):
                    if gain_row is None:
                        dve.tensor_scalar(xn[:, t, :], x[:, t, :], st[:, 4 + t:5 + t], None, ALU.mult).then_inc(xn_ready, 1)
                    else:
                        to = gain_row[1]
                        link(dve.scalar_tensor_tensor(out=to[:, t, :], in0=x[:, t, :], scalar=st[:, 4 + t:5 + t], in1=gain_row[0],
                                                      op0=ALU.mult, op1=ALU.mult))
                C.norm += 1
                C.xn += 2

            def tr_copy(C, dst, scale=None, shift=None):
                dve.wait_ge(tr_done, C.tr + 1)
                for b in range(2):
                    src = psT[:, C.tr % 2, b * S:(b + 1) * S]
                    if scale is None:
                        ins = dve.tensor_copy(dst(b), src)
                    elif shift is None:
                        ins = dve.tensor_scalar(dst(b), src, scale(b), None, ALU.mult)
                    else:
                        ins = dve.tensor_scalar(dst(b), src, scale(b), shift(b), ALU.mult, ALU.add)
                ins.then_inc(tr_used, 1)
                C.tr += 1

            def tr_all(C, scale=None, shift=None):
                for k in range(0, KC, 2):
                    tr_copy(C, lambda b: xT[:, k + b, :],
                            None if scale is None else (lambda b: scale[:, k + b:k + b + 1]),
                            None if shift is None else (lambda b: shift[:, k + b:k + b + 1]))

            def residual(C, gates):
                for n in range(2):
                    dve.wait_ge(lin_done, C.lin + 1)
                    pair = 2 * (C.lin % 2)
                    for t in range(NT):
                        xs = x[:, t, n * UC:(n + 1) * UC]
                        if gates is not None:
                            tmp = xn[:, t, n * UC:(n + 1) * UC]
                            link(dve.tensor_tensor(tmp, lin[:, pair + t, :], gates[:, n * UC:(n + 1) * UC], ALU.mult))
                            ins = dve.tensor_tensor(xs, xs, tmp, ALU.add)
                        else:
                            ins = dve.tensor_tensor(xs, xs, lin[:, pair + t, :], ALU.add)
                    ins.then_inc(lin_used, 1)
                    C.lin += 1
                dve.wait_ge(lin_used, C.lin)
                dve.sem_inc(x_ready, 1)
                C.x += 1

            def attention(C, m):
                dve.wait_ge(qk_ready, 1)
                for b in range(0, m.nblk, 2):
                    if b < 8:
                        tr_copy(C, lambda c: qkT[:, b + c, :], lambda c: m.scale)
                    else:
                        tr_copy(C, lambda c: qkT[:, b + c, :])
                for i in range(m.nsub + 4):
                    if i < m.nsub:
                        g = C.sc + i
                        dve.wait_ge(sc_done, g + 1)
                        if g >= 2:
                            dve.wait_ge(ex_done, g - 1)
                        for t in range(NT):
                            mask = cst(m.mask)[:, t * S:(t + 1) * S]
                            ins = dve.tensor_tensor_reduce(sm[:, g % 2, t, :], psS[:, g % 2, t * S:(t + 1) * S], mask, 1.0, -3e38,
                                                           ALU.add, ALU.max, st[:, 10 + t:11 + t])
                        ins.then_inc(sc_used, 1)
                        dve.wait_ge(sc_used, g + 1)
                        nm = st[:, 12 + 2 * (g % 2):14 + 2 * (g % 2)]
                        if m is SWA:
                            ins = dve.tensor_scalar(nm, st[:, 10:12], sinks[:, i:i + 1], -1.0, ALU.max, ALU.mult)
                        else:
                            ins = dve.tensor_scalar(nm, st[:, 10:12], -1.0, None, ALU.mult)
                        ins.then_inc(sm_max, 1)
                        dve.wait_ge(sm_max, g + 1)
                    if 0 <= i - 1 < m.nsub:
                        probs(C, m, i - 1)
                    if m.head_at(i, 3) is not None:
                        heads(C, m, m.head_at(i, 3))
                C.sc += m.nsub
                C.out += m.nout

            def heads(C, m, o):
                g = C.out + o
                dve.wait_ge(pv_done, g + 1)
                dve.tensor_copy(tokb[:, :, o * m.width:(o + 1) * m.width],
                                lin[:, g % 2, 0:NT * m.width].rearrange("p (t w) -> p t w", t=NT)).then_inc(pv_used, 1)

            def probs(C, m, s):
                g = C.sc + s
                o = C.out + s // m.join
                dve.wait_ge(ex_done, g + 1)
                r = st[:, 16 + 2 * (g % 2):18 + 2 * (g % 2)]
                if m is SWA:
                    link(dve.tensor_tensor(r, r, st[:, 20 + 2 * (g % 2):22 + 2 * (g % 2)], ALU.add))
                link(dve.reciprocal(r, r))
                if m is DIFF and s % 2 == 1:
                    link(dve.tensor_scalar(r, r, st[:, 60:61], None, ALU.mult))
                for t in range(NT):
                    rt = st[:, 16 + 2 * (g % 2) + t:17 + 2 * (g % 2) + t]
                    if m is not DIFF:
                        ins = dve.tensor_scalar(pr[:, g % 2, t, :], pr[:, g % 2, t, :], rt, None, ALU.mult)
                    elif s % 2 == 0:
                        if t == 0 and o >= 2:
                            dve.wait_ge(pt_done, o - 1)
                        ins = dve.tensor_scalar(pr[:, o % 2, t, :], rope_t[:, 2 * (g % 2) + t, 0:S], rt, None, ALU.mult)
                    else:
                        ins = dve.scalar_tensor_tensor(out=pr[:, o % 2, t, :], in0=rope_t[:, 2 * (g % 2) + t, 0:S], scalar=rt,
                                                       in1=pr[:, o % 2, t, :], op0=ALU.mult, op1=ALU.add)
                if s % m.join == m.join - 1:
                    ins.then_inc(pn_done, 1)
                    dve.wait_ge(pn_done, o + 1)
                else:
                    link(ins)

            def head_rms(src, heads, lo, ready):
                for t in range(NT):
                    for name, (a, n) in enumerate(heads):
                        sq = xn[:, t, 0:n * P]
                        link(dve.tensor_tensor(sq, src[:, t, a:a + n * P], src[:, t, a:a + n * P], ALU.mult))
                        link(dve.tensor_reduce(st[:, lo:lo + n], sq.rearrange("p (h d) -> p h d", d=P), AX, ALU.add))
                        lo += n
                r = st[:, 24:lo]
                link(dve.tensor_scalar(r, r, 1.0 / P, EPS, ALU.mult, ALU.add))
                link(dve.reciprocal(r, r))
                dve.sem_inc(hn_sq, 1)
                dve.wait_ge(hn_rs, ready)

            dve.wait_ge(s_const, 32)
            dve.memset(base_f[:, :], 0.0).then_inc(pchain, 1)
            dve.wait_ge(pchain, 1)
            with dve.Fori(0, DEPTH) as l:
                C = Counts()
                chain[0] = 0
                dve.wait_ge(p_tr, 1)
                link(dve.memset(ones, 1.0))
                dve.tensor_copy(pcol[:, 0:76], psT[:, 0, 0:76]).then_inc(p_col, 1)
                dve.wait_ge(p_col, 1)
                dve.wait_ge(s_cact, 1)
                slots = Counts()
                for n in range(N_ADA * D // UC):
                    slot, landed = slots.next_slot()
                    dve.wait_ge(ld[slot], landed)
                    if n >= 2:
                        dve.wait_ge(s_ada, n - 1)
                    acc = ada_acc[:, n % 2, :]
                    link(dve.tensor_scalar(acc, ring[:, slot, 0, :], cact[:, 0:1], None, ALU.mult))
                    for k in range(1, KC):
                        ins = dve.scalar_tensor_tensor(out=acc, in0=ring[:, slot, k, :], scalar=cact[:, k:k + 1], in1=acc,
                                                       op0=ALU.mult, op1=ALU.add)
                        if k < KC - 1:
                            link(ins)
                    ins.then_inc(acc_ready, 1)
                dve.wait_ge(s_ada, 12)
                dve.wait_ge(s_par, 16 * 10)
                dve.tensor_tensor(rowb[:, :, :].rearrange("p a d -> p (a d)"), rowb[:, :, :].rearrange("p a d -> p (a d)"),
                                  lin[:, :, :].rearrange("p b n -> p (b n)"), ALU.add).then_inc(s_gbc, 1)
                dve.wait_ge(s_gbc, 1)
                for lo in (0, 24):
                    link(dve.tensor_tensor(modc[:, lo:lo + 16], psS[:, 0, lo:lo + 16], pcol[:, lo:lo + 16], ALU.add))
                for a, w, scl in ((0, 48, 8), (1, 56, 32)):
                    link(dve.tensor_scalar(aff[:, a, :], modc[:, scl:scl + 8], 1.0, None, ALU.add))
                    link(dve.tensor_tensor(aff[:, a, :], aff[:, a, :], pcol[:, w:w + 8], ALU.mult))
                norm(C)
                tr_all(C, aff[:, 0, :], modc[:, 0:8])
                dve.wait_ge(lin_used, 3)
                head_rms(proj, ((0, NQ1), (D, NKV1)), 24, 1)
                for t in range(NT):
                    for h in range(NQ1 + NKV1):
                        sl = proj[:, t, h * P:(h + 1) * P]
                        gain = wrow[:, 0 if h < NQ1 else 1, :]
                        ins = dve.scalar_tensor_tensor(out=sl, in0=sl, scalar=st[:, 44 + 10 * t + h:45 + 10 * t + h],
                                                       in1=gain, op0=ALU.mult, op1=ALU.mult)
                    link(ins)
                    nh = NQ1 + NKV1
                    v = proj[:, t, 0:nh * P].rearrange("p (h r e f) -> p h r e f", r=2, e=2, f=32)
                    tmp = xn[:, :, :].rearrange("p t d -> p (t d)")
                    for r in range(2):
                        x1, x2 = v[:, :, r, 0, :], v[:, :, r, 1, :]
                        w = nh * 32
                        co = cst("cos")[:, t * 64 + r * 32:t * 64 + (r + 1) * 32].rearrange("p (a f) -> p a f", a=1).to_broadcast([P, nh, 32])
                        si = cst("sin")[:, t * 64 + r * 32:t * 64 + (r + 1) * 32].rearrange("p (a f) -> p a f", a=1).to_broadcast([P, nh, 32])
                        tt = [tmp[:, q * w:(q + 1) * w].rearrange("p (h f) -> p h f", f=32) for q in range(4)]
                        dve.tensor_tensor(tt[0], x1, co, ALU.mult)
                        dve.tensor_tensor(tt[1], x2, si, ALU.mult)
                        dve.tensor_tensor(tt[2], x2, co, ALU.mult)
                        link(dve.tensor_tensor(tt[3], x1, si, ALU.mult))
                        dve.tensor_tensor(x1, tt[0], tt[1], ALU.subtract)
                        link(dve.tensor_tensor(x2, tt[2], tt[3], ALU.add))
                dve.sem_inc(qk_ready, 1)
                C.lin += 8
                dve.wait_ge(lin_used, C.lin)
                attention(C, GQA)
                dve.wait_ge(pv_used, C.out)
                dve.sem_inc(tok_ready, 1)
                tr_all(C)
                for n in range(4):
                    dve.wait_ge(lin_done, C.lin + 1)
                    pair = 2 * (C.lin % 2)
                    cols = slice((n % 2) * UC, (n % 2 + 1) * UC)
                    gc = (2048 if n < 2 else 3072) + (n % 2) * UC
                    for t in range(NT):
                        to = xn[:, t, cols] if n < 2 else tokb[:, t, cols]
                        link(dve.tensor_tensor(to, lin[:, pair + t, :], proj[:, t, gc:gc + UC], ALU.mult))
                    dve.sem_inc(lin_used, 1)
                    C.lin += 1
                link(dve.tensor_tensor(xn[:, :, :], xn[:, :, :], tokb[:, :, :], ALU.add))
                dve.sem_inc(merged_ready, 1)
                tr_all(C)
                residual(C, rowb[:, 0, :])
                norm(C)
                tr_all(C, aff[:, 1, :], modc[:, 24:32])
                for t in range(NT):
                    for k in range(0, KC, 4):
                        tr_copy(C, lambda b: tokb[:, t, (k + 2 * b) * P:(k + 2 * b + 2) * P])

                dve.sem_inc(u_free, GB)

                def top16(src, work, n, v, iu):
                    link(dve.max(v[:, 0:8], src))
                    link(dve.max_index(iu[:, 0:8], v[:, 0:8], src))
                    link(dve.match_replace(work, v[:, 0:8], src, -3e38))
                    link(dve.max(v[:, 8:16], work))
                    link(dve.max_index(iu[:, 8:16], v[:, 8:16], work))

                def topk(h, j, t):
                    cb = NT * j + t
                    restart_chain()
                    if t == 0:
                        wait_loop(dve, ps_done, h + 1)
                        link(dve.tensor_copy(topb[:, :, 0, :], psS[:, 1, :].rearrange("p (a n) -> p a n", n=NKEY)))
                        dve.sem_inc(ps_used, 1)
                    for q in range(2):
                        top16(topb[:, 2 * t + q, 0, :], topb[:, 2 * t + q, 1, :], NKEY, vals[:, q, :], idxu[:, q, :])
                    link(dve.tensor_copy(idxf[:, :, :], idxu[:, :, :]))
                    grid = [P, TOPK, TOPK]

                    def down(a):
                        return a.rearrange("p (a b) -> p a b", b=1).to_broadcast(grid)

                    def along(a):
                        return a.rearrange("p (a b) -> p a b", a=1).to_broadcast(grid)

                    def m(q):
                        return sc2[:, q, :].rearrange("p (a b) -> p a b", a=TOPK)

                    link(dve.tensor_tensor(m(0), down(vals[:, 0, :]), along(vals[:, 1, :]), ALU.add))
                    if not (isinstance(h, int) and h < 2):
                        wait_loop(dve, v_free, h * 32 + (16 * t + 16 + V0 - 64), alone=True)
                    top16(sc2[:, 0, :], sc2[:, 1, :], 256, tops[:, cb, :], posu[:, 0, :])
                    link(dve.tensor_scalar(nmx[:, cb, :], tops[:, cb, 0:1], -1.0, None, ALU.mult))
                    link(dve.tensor_scalar(posu[:, 1, :], posu[:, 0, :], 4, None, ALU.logical_shift_right))
                    link(dve.tensor_scalar(posu[:, 2, :], posu[:, 0, :], 15, None, ALU.bitwise_and))
                    link(dve.tensor_copy(posfl[:, 0:2, :], posu[:, 1:3, :]))
                    for q in range(2):
                        link(dve.tensor_tensor(m(2 + q), down(posfl[:, q, :]), along(cst("iota")), ALU.is_equal))
                        link(dve.tensor_tensor(m(4 + q), m(2 + q), along(idxf[:, q, :]), ALU.mult))
                        link(dve.tensor_reduce(posfl[:, 2 + q, :], m(4 + q), AX, ALU.add))
                    link(dve.scalar_tensor_tensor(out=posfl[:, 0, :], in0=posfl[:, 2, :], scalar=float(NKEY), in1=posfl[:, 3, :],
                                                  op0=ALU.mult, op1=ALU.add))
                    link(dve.tensor_scalar(eidx[:, cb, :], posfl[:, 0, :], base_f[:, 0:1], None, ALU.add))
                    dve.sem_inc(idx_ready, 1)

                def dots(h, j, t):
                    cb = NT * j + t
                    c = (h - j) * 2 + cb
                    for k in range(TOPK):
                        n = 16 * cb + k
                        wait_loop(dve, u_ld[n % GB], l * LANDED + (h - j) * 64 + 16 * (n // GB + 1))
                        dve.tensor_tensor_reduce(ubuf[:, n % GB, :], ubuf[:, n % GB, :], tokb[:, t, :], 1.0, 0.0,
                                                 ALU.mult, ALU.add, hdot[:, cb, k:k + 1]).then_inc(h_ready, 1)
                    wait_loop(dve, gate_ready, c + 1, alone=True)
                    restart_chain()
                    link(dve.reciprocal(ers[:, cb, 1:2], ers[:, cb, 0:1]))
                    wait_loop(dve, gelu_ready, c + 1)
                    link(dve.scalar_tensor_tensor(out=actw[:, cb, :], in0=eg[:, cb, :], scalar=ers[:, cb, 1:2], in1=gel[:, cb, :],
                                                  op0=ALU.mult, op1=ALU.mult))
                    dve.sem_inc(w_ready, 1)

                for t in range(NT):
                    topk(0, 0, t)
                with dve.Fori(0, PH // 2 - 1) as hp:
                    for j in range(2):
                        for t in range(NT):
                            dots(2 * hp + j, j, t)
                            topk(2 * hp + j + 1, 1 - j, t)
                for t in range(NT):
                    dots(PH - 2, 0, t)
                    topk(PH - 1, 1, t)
                for t in range(NT):
                    dots(PH - 1, 1, t)
                restart_chain()
                link(dve.tensor_scalar(base_f[:, :], base_f[:, :], float(NEXP), None, ALU.add))
                residual(C, rowb[:, 1, :])
                layer_end(dve, l)

            C = Counts()
            chain[0] = 0
            dve.wait_ge(s_par, 128)
            dve.wait_ge(p_tr, 1)
            dve.tensor_copy(pcol[:, 0:64], psT[:, 0, 0:64]).then_inc(p_col, 1)
            link(dve.tensor_copy(posf[:, :], posi[:, :]))
            for t in range(NT):
                ins = dve.tensor_scalar(ang[:, 0, t, :], cst("inv"), posf[:, t:t + 1], None, ALU.mult)
            link(ins)
            TWO_PI = 2.0 * np.pi
            PARTS = [6.28125, float(np.float32(TWO_PI - 6.28125).view(np.uint32) & np.uint32(0xFFFFF000)) * 0]
            c1 = 6.28125
            c2 = float(np.array(np.array([TWO_PI - c1], np.float32).view(np.uint32) & np.uint32(0xFFFFF000)).view(np.float32)[0])
            c3 = float(np.float32(TWO_PI - c1 - c2))
            ROUND = 12582912.0
            for q, quarter in ((0, 0.25), (1, 0.0)):
                a, k, r = ang[:, 0, :, :], ang[:, 1, :, :], ang[:, 4 + q, :, :]
                link(dve.tensor_scalar(k, a, 1.0 / TWO_PI, quarter, ALU.mult, ALU.add))
                link(dve.tensor_scalar(k, k, ROUND, None, ALU.add))
                link(dve.tensor_scalar(k, k, -ROUND, None, ALU.add))
                link(dve.scalar_tensor_tensor(out=r, in0=k, scalar=-c1, in1=a, op0=ALU.mult, op1=ALU.add))
                link(dve.scalar_tensor_tensor(out=r, in0=k, scalar=-c2, in1=r, op0=ALU.mult, op1=ALU.add))
                link(dve.scalar_tensor_tensor(out=r, in0=k, scalar=-c3, in1=r, op0=ALU.mult, op1=ALU.add))
                if quarter:
                    link(dve.tensor_scalar(r, r, float(np.pi / 2), None, ALU.add))
                link(dve.tensor_scalar(r, r, 3.1415925, -3.1415925, ALU.min, ALU.max))
            dve.sem_inc(rope_arg, 1)
            norm(C, (rowb[:, 0, :], x))
            dve.sem_inc(x_ready, 1)
            C.xn = 0
            C.x = 1
            dve.wait_ge(rope_cs, 1)
            for i, m in enumerate(MIXERS2):
                slot = i // 3
                if m is DIFF:
                    dve.wait_ge(lam_e, 64 * (slot + 1))
                    for q in range(2):
                        link(dve.tensor_tensor_reduce(lamv[:, 2 * q, :], lamv[:, 2 * q, :], lamv[:, 2 * q + 1, :], 1.0, 0.0,
                                                      ALU.mult, ALU.add, st[:, 6 + q:7 + q]))
                    dve.sem_inc(lam_x, 1)
                    dve.wait_ge(lam_x, 3 * slot + 2)
                    link(dve.tensor_tensor(st[:, 60:61], st[:, 9:10], st[:, 8:9], ALU.subtract))
                    link(dve.tensor_scalar(st[:, 60:61], st[:, 60:61], -LAM_INIT[i], None, ALU.add))
                    dve.sem_inc(lam_x, 1)
                norm(C)
                tr_all(C, pcol[:, 8 * i:8 * i + 8])
                if m is SWA:
                    w = SWA_IN // NSWA
                    for n in range(NSWA):
                        dve.wait_ge(lin_done, C.lin + 1)
                        pair = 2 * (C.lin % 2)
                        for t in range(NT):
                            ins = dve.tensor_tensor(proj[:, t, n * w:(n + 1) * w], lin[:, pair + t, 0:w], bias_row[:, n * w:(n + 1) * w], ALU.add)
                        link(ins)
                        dve.sem_inc(lin_used, 1)
                        C.lin += 1
                    nh = 18
                else:
                    dve.wait_ge(lin_used, C.lin + 4)
                    C.lin += 6
                    nh = 32
                for t in range(NT):
                    v = proj[:, t, 0:nh * HD2].rearrange("p (h d) -> p h d", d=HD2)
                    x1, x2 = v[:, :, 0:8], v[:, :, 8:16]
                    co = cs2[:, 0, t, :].rearrange("p (a f) -> p a f", a=1).to_broadcast([P, nh, 8])
                    si = cs2[:, 1, t, :].rearrange("p (a f) -> p a f", a=1).to_broadcast([P, nh, 8])
                    tt = [rope_t[:, q, 0:nh * 8].rearrange("p (h f) -> p h f", f=8) for q in range(4)]
                    dve.tensor_tensor(tt[0], x1, co, ALU.mult)
                    dve.tensor_tensor(tt[1], x2, si, ALU.mult)
                    dve.tensor_tensor(tt[2], x2, co, ALU.mult)
                    link(dve.tensor_tensor(tt[3], x1, si, ALU.mult))
                    dve.tensor_tensor(x1, tt[0], tt[1], ALU.subtract)
                    link(dve.tensor_tensor(x2, tt[2], tt[3], ALU.add))
                if m is SWA:
                    for t in range(NT):
                        k3 = proj[:, t, D:D + 2 * HD2].rearrange("p (h d) -> p h d", d=HD2)
                        d3 = xn[:, t, 0:2 * P].rearrange("p (h r d) -> p h r d", r=2, d=HD2)
                        dve.tensor_copy(d3[:, :, 0, :], k3)
                        ins = dve.tensor_copy(d3[:, :, 1, :], k3)
                    link(ins)
                dve.sem_inc(qk_ready, 1)
                attention(C, m)
                dve.wait_ge(pv_used, C.out)
                if m is DIFF:
                    head_rms(tokb, ((0, 8),), 24, slot + 1)
                    for t in range(NT):
                        for h in range(8):
                            sl = tokb[:, t, h * P:(h + 1) * P]
                            ins = dve.scalar_tensor_tensor(out=sl, in0=sl, scalar=st[:, 44 + 8 * t + h:45 + 8 * t + h],
                                                           in1=wrow[:, slot, :], op0=ALU.mult, op1=ALU.mult)
                    link(ins)
                    link(dve.tensor_scalar(tokb[:, :, :], tokb[:, :, :], 1.0 - LAM_INIT[i], None, ALU.mult))
                dve.sem_inc(tok_ready, 1)
                tr_all(C)
                residual(C, None)
                norm(C)
                tr_all(C, pcol[:, 32 + 8 * i:40 + 8 * i])
                ub = i * 8

                def square(n, b, ab):
                    wait_loop(dve, rl_done, n + ub + 1)
                    wait_loop(dve, a_free, n + ub + 1)
                    src = proj[:, 1, b * 1024:(b + 1) * 1024]
                    dve.tensor_tensor(aT[:, b, :, :].rearrange("p f s -> p (f s)"), src, src, ALU.mult).then_inc(a_done, 1)

                for n in range(2):
                    square(n, n, n)
                with dve.Fori(1, 4) as r:
                    for b in range(2):
                        square(2 * r + b, b, b)
                dve.wait_ge(lin_done, C.lin + 2)
                residual(C, None)
            norm(C, (rowb[:, 1, :], xn))
            dve.sem_inc(xn_ready, 2)

        @block.gpsimd
        def _(pool):
            table = {"u": T["expert_u"].rearrange("l e d -> (l e) d"), "v": T["expert_v"].rearrange("l e d -> (l e) d")}
            with pool.Fori(0, DEPTH) as l:
                def gathers(hbase, j, t):
                    cb = NT * j + t
                    wait_loop(pool, idx_ready, hbase * 2 + cb + 1)
                    for which, buf, landed, in_use, credit in (("u", ubuf, u_ld, h_ready, u_free), ("v", vbuf, v_ld, v_free, None)):
                        for k in range(TOPK):
                            n = 16 * cb + k
                            if credit is None:
                                wait_loop(pool, in_use, hbase * 32 + (n + 1 + V0 - GB), alone=True)
                            elif isinstance(hbase, int) and hbase == 0:
                                if n >= GB:
                                    pool.wait_ge(in_use, n - GB + 1)
                            else:
                                wait_loop(pool, in_use, hbase * 32 + (n - GB + 1), alone=True)
                            pool.indirect_dma_start(
                                out=buf[:, n % GB, :], out_offset=None, in_=table[which],
                                in_offset=bass.IndirectOffsetOnAxis(ap=eidx[:, cb, k:k + 1], axis=0),
                            ).then_inc(landed[n % GB], 16)

                for j in range(2):
                    for t in range(NT):
                        gathers(0, j, t)
                with pool.Fori(1, PH // 2) as hp:
                    for j in range(2):
                        for t in range(NT):
                            gathers(2 * hp, j, t)
                layer_end(pool, l)


def kernel(**inputs):
    import concourse.bacc as _bacc
    from concourse.bass_utils import run_bass_kernel_spmd as _run

    nc = _bacc.Bacc("TRN2", target_bir_lowering=False, num_devices=1)
    arrays, tensors = {}, {}
    for name in INS1 + INS2:
        a = np.ascontiguousarray(inputs[name])
        arrays[f"in_{name}"] = a
        tensors[name] = nc.dram_tensor(f"in_{name}", a.shape, mybir.dt.from_np(a.dtype), kind="ExternalInput").ap()
    arrays["in_consts"] = const_table()
    tensors["consts"] = nc.dram_tensor("in_consts", (P, CW), F32, kind="ExternalInput").ap()
    out = nc.dram_tensor("out_0", (1, S, D), F32, kind="ExternalOutput").ap()
    program(nc, tensors, out)
    r = _run(nc, [arrays], core_ids=[0])
    return r.results[0]["out_0"]
```

```python
from contextlib import ExitStack

import concourse.bass as bass
import numpy as np
from concourse import mybir

F32 = mybir.dt.float32
F32R = mybir.dt.float32r
I32 = mybir.dt.int32
U32 = mybir.dt.uint32
ALU = mybir.AluOpType
ACT = mybir.ActivationFunctionType
AX = mybir.AxisListType.X

P = 128
D = 1024
S = 256
NT = S // P
KC = D // P
UC = 512
RING = 4
RING2 = 2
NPC = 4
DEPTH = 2
EPS = 1e-6
N_ADA = 6
HD1 = 128
NQ1, NKV1 = 8, 2
NPG = 4
PH = 8
NKEY = 128
NEXP = NKEY * NKEY
TOPK = 16
GB = 8
DB = 4
V0 = GB + 2 * NT * TOPK
LANDED = 16 * PH * NT * TOPK // GB
DEPTH2 = 4
HD2 = 64
ROT = 16
D_FF = 4096
SWA_IN = 1280
NSWA = 4
POOL_WINDOWS = (2, 4, 8, 16)

CONSTS = [("ident", 128), ("cos", 128), ("sin", 128), ("zero", 512), ("causal", 512),
          ("band", 512), ("pool", 2048), ("inv", 8), ("iota", 16)]
COFF = {}
CW = 0
for _n, _w in CONSTS:
    COFF[_n] = (CW, CW + _w)
    CW += _w


def const_table():
    t = np.zeros((P, CW), np.float32)

    def put(name, a):
        lo, hi = COFF[name]
        t[:, lo:hi] = a.reshape(P, hi - lo)

    put("ident", np.eye(P, dtype=np.float32))
    tok = np.arange(S)
    inv1 = (1.0 / (np.float32(10000.0) ** (np.arange(0, 64, 2, dtype=np.float32) / np.float32(64)))).astype(np.float32)
    ang = np.stack([(tok // 64).astype(np.float32)[:, None] * inv1,
                    (tok % 64).astype(np.float32)[:, None] * inv1], 1)
    for name, f in (("cos", np.cos), ("sin", np.sin)):
        a = f(ang.astype(np.float64)).astype(np.float32).reshape(NT, P, 64)
        put(name, a.transpose(1, 0, 2))
    q, k = tok[:, None], tok[None, :]
    for name, ok in (("causal", k <= q), ("band", (k <= q) & (q - k < 128))):
        m = np.where(ok, 0.0, -1e30).astype(np.float32).reshape(NT, P, S)
        put(name, m.transpose(1, 0, 2))
    pools = []
    for w in POOL_WINDOWS:
        lo = np.clip(tok - w // 2, 0, S)
        hi = np.clip(tok + w // 2, 0, S)
        m = ((k >= lo[:, None]) & (k < hi[:, None])) / (hi - lo)[:, None].astype(np.float64) - np.eye(S)
        pools.append(m.T.reshape(NT, P, S))
    put("pool", np.stack(pools).astype(np.float32).transpose(2, 0, 1, 3))
    put("inv", np.broadcast_to((np.float32(500000.0) ** (-np.arange(0, ROT, 2, dtype=np.float32) / np.float32(ROT))).astype(np.float32), (P, 8)))
    put("iota", np.broadcast_to(np.arange(16, dtype=np.float32), (P, 16)))
    return t


class Mixer:
    def __init__(self, nsub, join, width, vcol, kshare, vshare, nblk, scale, mask):
        self.nsub, self.join, self.width, self.vcol = nsub, join, width, vcol
        self.kshare, self.vshare, self.nblk, self.scale, self.mask = kshare, vshare, nblk, scale, mask
        self.nout = nsub // join

    def score_operands(self, s):
        if self.nsub == 8:
            return s, 8 + s // self.kshare, 0, 128
        c = s % 2
        return s // 2, 8 + s // self.kshare, 64 * c, 64 * c + 64

    def head_at(self, i, lag):
        d = i - self.join - lag
        return d // self.join if d >= 0 and d % self.join == 0 and d // self.join < self.nout else None

    def v_at(self, o):
        c = self.vcol + self.width * (o // self.vshare)
        return c, c + self.width


GQA = Mixer(8, 1, 128, 1280, 4, 4, 10, 128.0 ** -0.5, "zero")
DIFF = Mixer(16, 2, 128, 2048, 2, 1, 16, 0.125, "causal")
MOBA = Mixer(16, 1, 64, 2048, 2, 1, 16, 0.125, "causal")
SWA = Mixer(16, 1, 64, 1152, 8, 8, 10, 0.125, "band")
MIXERS2 = [DIFF, MOBA, SWA, DIFF]
LAM_INIT = [0.8 - 0.6 * float(np.exp(-0.3 * i)) for i in range(DEPTH2)]


class Counts:

    def __init__(self, ring=RING):
        self.ring = ring
        self.unit = 0
        self.lin = 0
        self.tr = 0
        self.norm = 0
        self.xn = 0
        self.x = 0
        self.xh = 0
        self.sc = 0
        self.out = 0
        self.slot = [0] * ring

    def next_slot(self):
        s = self.unit % self.ring
        self.unit += 1
        self.slot[s] += 1
        return s, 16 * self.slot[s]


INS1 = ["x", "c", "ada_w", "ada_b", "norm_mix_w", "w_in", "q_norm_w", "k_norm_w", "w_attn_o",
        "pool_mix_w", "pool_scale", "w_pool_o", "w_out", "norm_ffn_w", "w_query", "sub_keys",
        "expert_u", "expert_v", "final_norm_w"]
INS2 = ["positions_2", "attn_norm_g_2", "mlp_norm_g_2", "diff_w_in_2", "diff_w_out_2",
        "diff_lam_q1_2", "diff_lam_k1_2", "diff_lam_q2_2", "diff_lam_k2_2", "diff_subln_g_2",
        "moba_w_in_2", "moba_w_out_2", "swa_w_in_2", "swa_b_in_2", "swa_sinks_2", "swa_w_out_2",
        "mlp_w_up_2", "mlp_w_down_2", "final_norm_g_2"]


def program(nc, T, out):
    with ExitStack() as ctx:
        def sb(name, shape, dt=F32):
            return ctx.enter_context(nc.sbuf_tensor(name, shape, dt))

        def sem(name):
            return ctx.enter_context(nc.semaphore(name))

        ctx.enter_context(nc.allow_non_contiguous_dma(reason="small parameter vectors"))
        const = sb("const", [P, CW])

        def cst(name):
            lo, hi = COFF[name]
            return const[:, lo:hi]

        ident = cst("ident")
        x = sb("x_res", [P, NT, D])
        xn = sb("xn", [P, NT, D])
        xT_at = nc.sbuf_base
        xT = sb("xT", [P, KC, S])
        tokb = sb("tokb", [P, NT, D])
        proj_at = nc.sbuf_base
        proj = sb("proj", [P, NT, 4096])
        ring_at = nc.sbuf_base
        ring = sb("ring", [P, RING, KC, UC])
        vbuf_at = nc.sbuf_base
        vbuf = sb("vbuf", [P, GB, D])
        rowb = sb("rowb", [P, 2, D])
        prow = sb("prow", [P, P])
        pcol = sb("pcol", [P, P])
        modc = sb("modc", [P, 48])
        cact = sb("cact", [P, KC])
        aff = sb("aff", [P, 4, KC])
        wrow = sb("wrow", [P, 4, P])
        st = sb("st", [P, 64])
        sm = sb("sm", [P, 2, NT, S])
        pr = sb("pr", [P, 2, NT, S])
        pT = sb("pT", [P, 2, NT, S])
        rope_t = sb("rope_t", [P, 4, 256])
        cs2 = sb("cs2", [P, 2, NT, 8])
        ang = sb("ang", [P, 6, NT, 8])
        posi = sb("posi", [P, NT], I32)
        posf = sb("posf", [P, NT])
        sinks = sb("sinks", [P, 16])
        lamv = sb("lamv", [P, 4, HD2])
        vals = sb("vals", [P, 2, TOPK])
        idxu = sb("idxu", [P, 2, TOPK], U32)
        idxf = sb("idxf", [P, 2, TOPK])
        posu = sb("posu", [P, 3, TOPK], U32)
        posfl = sb("posfl", [P, 4, TOPK])
        base_f = sb("base_f", [P, 1])
        tops = sb("tops", [P, 4, TOPK])
        nmx = sb("nmx", [P, 4, 1])
        eidx = sb("eidx", [P, 4, TOPK], U32)
        hdot = sb("hdot", [P, 4, TOPK])
        gel = sb("gel", [P, 4, TOPK])
        eg = sb("eg", [P, 4, TOPK])
        ers = sb("ers", [P, 4, 2])
        actw = sb("actw", [P, 4, TOPK])

        lin = ctx.enter_context(nc.psum_tensor("lin", [P, 4, 512], F32))
        psT = ctx.enter_context(nc.psum_tensor("psT", [P, 2, 512], F32))
        psS = ctx.enter_context(nc.psum_tensor("psS", [P, 2, 512], F32))

        ubuf = proj[:, :, :].rearrange("p t (b d) -> p (t b) d", d=D)
        poolw = vbuf[:, 0:4, :]
        qkT = vbuf[:, 4:8, :].rearrange("p b (h s) -> p (b h) s", s=S)
        mT = pT[:, :, :, :].rearrange("p a b s -> p (a b) s")
        mixT = pr[:, :, :, :].rearrange("p a b s -> p (a b) s")
        qTx = sm[:, :, :, :].rearrange("p a b s -> p (a b) s")
        skT = pT[:, 0, :, :].rearrange("p a (b k) -> p (a b) k", k=NKEY)
        topb = rope_t[:, :, :].rearrange("p a (b n) -> p a b n", b=2)
        skn = ring[:, 2, 0:2, :].rearrange("p j (q d) -> p j q d", q=2)
        diag = ring[:, 3, 0, :].rearrange("p (b n) -> p b n", b=DB)
        mixw = vbuf[:, 7, 512:1024].rearrange("p (g n) -> p g n", g=NPG)
        ones = vbuf[:, 7, 0:P]
        ada_acc = proj[:, 0, 0:2 * UC].rearrange("p (a n) -> p a n", a=2)
        sc2 = xn[:, :, :].rearrange("p t (b n) -> p (t b) n", n=256)
        bias_row = vbuf[:, 0:2, :].rearrange("p a d -> p (a d)")
        aT = proj[:, 0, :].rearrange("p (b f s) -> p b f s", b=4, s=S)

        def split_tensor(name, shape, at):
            return nc.alloc_sbuf_tensor_at(name, shape, F32R, offset=at)

        ws = split_tensor("weights_split", [P, NPC, 2, D], ring_at + 2 * 4 * KC * UC)
        xh = split_tensor("xT_high", [P, KC, S], xT_at)
        xl = split_tensor("xT_low", [P, KC, S], vbuf_at + 2 * 4 * D)
        a_s = split_tensor("act_split", [P, 2, 2, 4 * S], proj_at)

        def rl(b):
            return proj[:, 1, b * 1024:(b + 1) * 1024]

        def raw_piece(slot, p, kind, w):
            if kind == "block":
                return ring[:, slot, :, p * P:(p + 1) * P]
            return ring[:, slot, :, :].rearrange("p k n -> p (k n)")[:, p * w:(p + 1) * w]

        def part(p, which, kind, w):
            a = ws[:, p, which, 0:w]
            return a.rearrange("p (k n) -> p k n", k=KC) if kind == "block" else a

        s_const = sem("const_loaded")
        s_par = sem("params_loaded")
        s_poolw = sem("pool_weights_loaded")
        ld = [sem(f"ring_slot_loaded{i}") for i in range(RING)]
        x_ready = sem("x_ready")
        n_sq = sem("norm_squares")
        n_rec = sem("norm_reciprocal")
        n_rstd = sem("norm_rstd")
        xn_ready = sem("xn_ready")
        tr_done = sem("transposed")
        tr_used = sem("transposes_copied")
        lin_done = sem("linear_done")
        lin_used = sem("linear_copied")
        p_tr = sem("params_transposed")
        p_col = sem("params_in_columns")
        s_cact = sem("c_activated")
        s_ada = sem("ada_done")
        s_mod = sem("mod_ready")
        acc_ready = sem("ada_partial_sums_ready")
        s_gbc = sem("gate_rows_copied")
        qk_ready = sem("qk_ready")
        hn_sq = sem("head_norm_mean_ready")
        hn_rs = sem("head_norm_rstd_ready")
        sc_done = sem("scores_done")
        sc_used = sem("scores_copied")
        sm_max = sem("score_max_ready")
        ex_done = sem("exp_done")
        pn_done = sem("probs_ready")
        pt_copied = sem("probs_transposed_copied")
        pt_done = sem("probs_transposed")
        pv_done = sem("heads_done")
        pv_used = sem("heads_copied")
        pl_mm = sem("pool_matmuls")
        pl_cp = sem("pool_copied")
        tok_ready = sem("attention_rows_ready")
        merged_ready = sem("merged_ready")
        xf_ready = sem("xf_rows_ready")
        sk_ld = [sem(f"sub_keys_loaded{i}") for i in range(2)]
        sk_done = sem("sub_keys_transposed")
        sk_used = sem("sub_keys_copied")
        q_done = sem("peer_query_done")
        q_used = sem("peer_query_copied")
        ps_done = sem("peer_scores_done")
        ps_used = sem("peer_scores_copied")
        idx_ready = sem("expert_indices_ready")
        u_ld = [sem(f"u_rows_landed{i}") for i in range(GB)]
        v_ld = [sem(f"v_rows_landed{i}") for i in range(GB)]
        u_free = sem("u_buffer_free")
        v_free = sem("v_buffer_free")
        h_ready = sem("expert_dots_ready")
        gate_ready = sem("router_exp_ready")
        gelu_ready = sem("gelu_ready")
        w_ready = sem("expert_weights_ready")
        dg_done = sem("diag_ready")
        y_open = sem("y_opened")
        up_done = sem("mlp_up_done")
        rl_done = sem("relu_done")
        a_done = sem("mlp_act_ready")
        a_free = sem("mlp_act_buffer_free")
        hi_ready = sem("piece_high_ready")
        lo_ready = sem("piece_low_ready")
        pc_used = sem("piece_used")
        xh_ready = sem("xT_high_ready")
        sq_done = sem("relu_squared")
        ahi_done = sem("act_high_ready")
        lam_e = sem("lambda_exponents")
        lam_x = sem("lambda_exps")
        rope_arg = sem("rope_args_ready")
        rope_cs = sem("rope_tables_ready")
        dchain = sem("dve_step")
        achain = sem("act_step")
        pchain = sem("pool_step")
        s_out = sem("output_stored")
        arrive = sem("layer_arrived")
        go = sem("layer_go")
        waits_met = sem("waits_met")
        cleared = [ld, sk_ld, [s_par, s_poolw, x_ready, n_sq, n_rec, n_rstd,
                   xn_ready, tr_done, tr_used, lin_done, lin_used, p_tr, p_col, s_cact, s_ada,
                   s_mod, acc_ready, s_gbc, qk_ready, hn_sq, hn_rs, sc_done, sc_used, sm_max,
                   ex_done, pn_done, pt_copied, pt_done, pv_done, pv_used, pl_mm, pl_cp, tok_ready,
                   merged_ready, xf_ready, sk_done, sk_used, q_done, q_used, ps_done, ps_used,
                   idx_ready, u_free, v_free, h_ready, gate_ready, gelu_ready, w_ready, 
                   dg_done, y_open, up_done, rl_done, a_done, a_free, dchain, achain]]

        def wait_loop(eng, s, value, alone=False):
            eng.wait_ge(s, value)
            if alone and not isinstance(value, int):
                eng.sem_inc(waits_met, 1)

        def layer_end(eng, l):
            eng.sem_inc(arrive, 1)
            wait_loop(eng, go, l + 1)

        block = ctx.enter_context(nc.Block())

        @block.sync
        def _(sp):
            sp.dma_start(const[:, :], T["consts"]).then_inc(s_const, 16)
            sp.dma_start(x[:, :, :], T["x"][0].rearrange("(t p) d -> p t d", p=P)).then_inc(s_const, 16)

            used = []

            def unit(C, src, used_up, kc=KC, cols=UC):
                n = C.unit
                slot, _ = C.next_slot()
                if n >= RING:
                    sp.wait_ge(*used[n - RING])
                used.append(used_up)
                dst = ring[:, slot, :, :].rearrange("p k n -> p (k n)")[:, 0:kc * cols]
                sp.dma_start(dst.rearrange("p (k n) -> p k n", k=kc), src).then_inc(ld[slot], 16)

            def cols_of(w, lo, n):
                return w.rearrange("(k p) n -> p k n", p=P)[:, :, lo:lo + n]

            with sp.Fori(0, DEPTH) as l:
                C = Counts()
                used.clear()
                sp.dma_start(prow[0:48, :], T["ada_b"][l].rearrange("(r j) -> r j", j=P)).then_inc(s_par, 16)
                sp.dma_start(prow[48:56, :], T["norm_mix_w"][l].rearrange("(r j) -> r j", j=P)).then_inc(s_par, 16)
                sp.dma_start(prow[56:64, :], T["norm_ffn_w"][l].rearrange("(r j) -> r j", j=P)).then_inc(s_par, 16)
                sp.dma_start(prow[64:72, :], T["c"].rearrange("a (r j) -> (a r) j", j=P)).then_inc(s_par, 16)
                sp.dma_start(prow[72:76, :], T["pool_scale"][l].rearrange("(r j) -> r j", j=P)).then_inc(s_par, 16)
                sp.dma_start(wrow[:, 0, :], T["q_norm_w"][l].rearrange("(a d) -> a d", a=1).to_broadcast([P, HD1])).then_inc(s_par, 16)
                sp.dma_start(wrow[:, 1, :], T["k_norm_w"][l].rearrange("(a d) -> a d", a=1).to_broadcast([P, HD1])).then_inc(s_par, 16)
                sp.dma_start(mixw[:, :, :], T["pool_mix_w"][l].rearrange("g c d -> c g d")).then_inc(s_par, 16)
                for g in range(2):
                    lo = (3 * g + 2) * D
                    sp.dma_start(rowb[:, g, :], T["ada_b"][l][lo:lo + D].rearrange("(a d) -> a d", a=1).to_broadcast([P, D])).then_inc(s_par, 16)
                for n in range(N_ADA * D // UC):
                    unit(C, cols_of(T["ada_w"][l], n * UC, UC), (acc_ready, n + 1))
                sp.dma_start(poolw, T["w_pool_o"][l].rearrange("(k p) n -> p k n", p=P)).then_inc(s_poolw, 16)
                for n in range(8):
                    unit(C, cols_of(T["w_in"][l], n * UC, UC), (lin_done, n + 1))
                for n in range(2):
                    unit(C, cols_of(T["w_attn_o"][l], n * UC, UC), (lin_done, n + 9))
                for n in range(2):
                    unit(C, cols_of(T["w_out"][l], n * UC, UC), (lin_done, n + 13))
                def head_loads(h, j, first):
                    if first:
                        sp.wait_ge(lin_done, 14)
                    else:
                        wait_loop(sp, q_done, h - 1)
                    sp.dma_start(ring[:, j, :, :], cols_of(T["w_query"][l], h * UC, UC)
                                 if isinstance(h, int) else
                                 T["w_query"][l].rearrange("(k p) (h n) -> h p k n", p=P, n=UC)[h]).then_inc(ld[j], 16)
                    if not first:
                        wait_loop(sp, sk_done, h - 1)
                    sp.dma_start(skn[:, j, :, :], T["sub_keys"][l].rearrange("h q n d -> h n q d")[h]).then_inc(sk_ld[j], 16)

                head_loads(0, 0, True)
                head_loads(1, 1, True)
                with sp.Fori(1, PH // 2) as hp:
                    for j in range(2):
                        head_loads(2 * hp + j, j, False)
                sp.wait_ge(x_ready, 2)
                wait_loop(sp, arrive, 4 * l + 4, alone=True)
                for group in cleared:
                    for s in group:
                        sp.sem_clear(s)
                sp.sem_inc(go, 1)

            C = Counts(RING2)
            sp.dma_start(rowb[:, 0, :], T["final_norm_w"].rearrange("(a d) -> a d", a=1).to_broadcast([P, D])).then_inc(s_par, 16)
            sp.dma_start(rowb[:, 1, :], T["final_norm_g_2"].rearrange("(a d) -> a d", a=1).to_broadcast([P, D])).then_inc(s_par, 16)
            sp.dma_start(prow[0:32, :], T["attn_norm_g_2"].rearrange("l (r j) -> (l r) j", j=P)).then_inc(s_par, 16)
            sp.dma_start(prow[32:64, :], T["mlp_norm_g_2"].rearrange("l (r j) -> (l r) j", j=P)).then_inc(s_par, 16)
            sp.dma_start(posi[:, :], T["positions_2"].rearrange("a (t p) -> p (a t)", p=P)).then_inc(s_par, 16)
            sp.dma_start(wrow[:, 0:2, :], T["diff_subln_g_2"].rearrange("(a l) d -> a l d", a=1).to_broadcast([P, 2, P])).then_inc(s_par, 16)
            sp.dma_start(sinks[:, :], T["swa_sinks_2"].to_broadcast([P, 16])).then_inc(s_par, 16)
            sp.dma_start(bias_row[:, 0:SWA_IN], T["swa_b_in_2"].to_broadcast([P, SWA_IN])).then_inc(s_par, 16)
            for i, m in enumerate(MIXERS2):
                slot = i // 3
                if m is DIFF:
                    if slot:
                        sp.wait_ge(lam_x, 1)
                    for v, name in enumerate(("q1", "k1", "q2", "k2")):
                        sp.dma_start(lamv[:, v, :], T[f"diff_lam_{name}_2"][slot:slot + 1, :].to_broadcast([P, HD2])).then_inc(lam_e, 16)
                w_in, w_o, n_in, cols = {0: (T["diff_w_in_2"], T["diff_w_out_2"], 6, UC),
                                         1: (T["moba_w_in_2"], T["moba_w_out_2"], 6, UC),
                                         2: (T["swa_w_in_2"], T["swa_w_out_2"], NSWA, SWA_IN // NSWA)}[i % 3]

                def unit2(src, kc=KC, cols=UC):
                    slot, _ = C.next_slot()
                    if C.unit > RING2:
                        sp.wait_ge(lo_ready, NPC * (C.unit - RING2))
                    dst = ring[:, slot, :, :].rearrange("p k n -> p (k n)")[:, 0:kc * cols]
                    sp.dma_start(dst.rearrange("p (k n) -> p k n", k=kc), src).then_inc(ld[slot], 16)

                for n in range(n_in):
                    unit2(cols_of(w_in[slot], n * cols, cols), cols=cols)
                for n in range(2):
                    unit2(cols_of(w_o[slot], n * UC, UC))
                up = T["mlp_w_up_2"][i].rearrange("(k p) (f n) -> f p k n", p=P, n=UC)
                down = T["mlp_w_down_2"][i].rearrange("(f k p) n -> f p k n", p=P, k=4)
                unit2(up[0])
                unit2(up[1])
                u0 = C.unit
                with sp.Fori(0, 3) as r:
                    for k, src in enumerate((down[2 * r], up[2 * r + 2], down[2 * r + 1], up[2 * r + 3])):
                        wait_loop(sp, lo_ready, 16 * r + NPC * (u0 + k - RING2 + 1))
                        at = (u0 + k) % RING2
                        dst = ring[:, at, :, :].rearrange("p k n -> p (k n)")
                        sp.dma_start(dst.rearrange("p (k n) -> p k n", k=KC if k % 2 else 4), src).then_inc(ld[at], 16)
                for _ in range(12):
                    C.next_slot()
                unit2(down[6], kc=4, cols=D)
                unit2(down[7], kc=4, cols=D)
            sp.wait_ge(xn_ready, 4 * 2 * DEPTH2 // 2 + 2)
            sp.dma_start(out[0].rearrange("(t p) d -> p t d", p=P), xn[:, :, :]).then_inc(s_out, 16)
            sp.wait_ge(s_out, 16)

        @block.tensor
        def _(pe):
            def tr_group(C, srcs):
                if C.tr >= 2:
                    pe.wait_ge(tr_used, C.tr - 1)
                for n, src in enumerate(srcs):
                    mm = pe.transpose(psT[:, C.tr % 2, n * P:(n + 1) * P], src, ident)
                mm.then_inc(tr_done, 1)
                C.tr += 1

            def tr_all(C, buf):
                for k in range(0, KC, 2):
                    tr_group(C, [buf[:, t, (k + b) * P:(k + b + 1) * P] for b in range(2) for t in range(NT)])

            def norm(C):
                C.norm += 1
                C.xn += 2
                pe.wait_ge(xn_ready, C.xn)
                tr_all(C, xn)

            def linear(C, lhs, kc, rhs, cols):
                pair = 2 * (C.lin % 2)
                if C.lin >= 2:
                    pe.wait_ge(lin_used, C.lin - 1)
                for t in range(NT):
                    for k in range(kc):
                        mm = pe.matmul(lin[:, pair + t, 0:cols], lhs[:, k, t * P:(t + 1) * P], rhs[:, k, :],
                                       start=(k == 0), stop=(k == kc - 1))
                C.lin += 1
                return mm.then_inc(lin_done, 1)

            def linear_units(C, lhs, n, cols=UC):
                for _ in range(n):
                    slot, landed = C.next_slot()
                    pe.wait_ge(ld[slot], landed)
                    w = ring[:, slot, :, :].rearrange("p k n -> p (k n)")[:, 0:KC * cols].rearrange("p (k n) -> p k n", k=KC)
                    linear(C, lhs, KC, w, cols)

            def attention(C, m):
                pe.wait_ge(lin_used, C.lin)
                tr0 = C.tr
                if C.tr:
                    pe.wait_ge(tr_used, C.tr)
                for b in range(0, m.nblk, 2):
                    srcs = []
                    for blk in (b, b + 1):
                        for t in range(NT):
                            if m is SWA and blk >= 8:
                                srcs.append(xn[:, t, (blk - 8) * P:(blk - 7) * P])
                            else:
                                srcs.append(proj[:, t, blk * P:(blk + 1) * P])
                    tr_group(C, srcs)
                pe.wait_ge(tr_used, C.tr)
                for i in range(m.nsub + 3):
                    if i < m.nsub:
                        g = C.sc + i
                        qb, kb, lo, hi = m.score_operands(i)
                        if g >= 2:
                            pe.wait_ge(sc_used, g - 1)
                        for t in range(NT):
                            mm = pe.matmul(psS[:, g % 2, t * S:(t + 1) * S], qkT[lo:hi, qb, t * P:(t + 1) * P],
                                           qkT[lo:hi, kb, :], start=True, stop=True)
                        mm.then_inc(sc_done, 1)
                    o = m.head_at(i, 1)
                    if o is not None:
                        g = C.out + o
                        pe.wait_ge(pn_done, g + 1)
                        if g >= 2:
                            pe.wait_ge(pt_copied, g - 1)
                        for kt in range(NT):
                            for t in range(NT):
                                mm = pe.transpose(psT[:, g % 2, kt * S + t * P:kt * S + (t + 1) * P],
                                                  pr[:, g % 2, t, kt * P:(kt + 1) * P], ident)
                        mm.then_inc(pt_done, 1)
                    o = m.head_at(i, 2)
                    if o is not None:
                        values(C, m, o)
                C.sc += m.nsub
                C.out += m.nout

            def values(C, m, o):
                g = C.out + o
                pe.wait_ge(pt_copied, g + 1)
                if g >= 2:
                    pe.wait_ge(pv_used, g - 1)
                a, b = m.v_at(o)
                for t in range(NT):
                    for kt in range(NT):
                        mm = pe.matmul(lin[:, g % 2, t * m.width:(t + 1) * m.width],
                                       pT[:, g % 2, kt, t * P:(t + 1) * P], proj[:, kt, a:b],
                                       start=(kt == 0), stop=(kt == NT - 1))
                mm.then_inc(pv_done, 1)

            pe.wait_ge(s_const, 32)
            with pe.Fori(0, DEPTH) as l:
                C = Counts()
                pe.wait_ge(s_par, 160)
                pe.transpose(psT[:, 0, 0:76], prow[0:76, :], ident[0:76, 0:76]).then_inc(p_tr, 1)
                for n in range(N_ADA * D // UC):
                    C.next_slot()
                    pe.wait_ge(acc_ready, n + 1)
                    acc = ada_acc[:, n % 2, :]
                    if n // 2 % 3 == 2:
                        mm = pe.matmul(lin[:, 2 * (n // 6) + n % 2, :], ones, acc, start=True, stop=True)
                    else:
                        for j in range(4):
                            mm = pe.matmul(psS[:, 0, 4 * n + j:4 * n + j + 1], acc[:, j * P:(j + 1) * P], ones[:, 0:1],
                                           start=True, stop=True)
                    mm.then_inc(s_ada, 1)
                pe.wait_ge(s_gbc, 1)
                C.tr = 0
                norm(C)
                pe.wait_ge(tr_used, C.tr)
                for n in range(8):
                    slot, landed = C.next_slot()
                    pe.wait_ge(ld[slot], landed)
                    linear(C, xT, KC, ring[:, slot, :, :], UC)
                pe.wait_ge(qk_ready, 1)
                attention(C, GQA)
                pe.wait_ge(pt_copied, C.out)
                pe.wait_ge(pv_used, C.out)
                for g in range(NPG):
                    for kt in range(NT):
                        lo = COFF["pool"][0] + (g * NT + kt) * S
                        mm = pe.matmul(psS[:, g // 2, (g % 2) * S:(g % 2 + 1) * S],
                                       proj[:, kt, 1536 + g * P:1536 + (g + 1) * P], const[:, lo:lo + S],
                                       start=(kt == 0), stop=(kt == NT - 1))
                mm.then_inc(pl_mm, 1)
                pe.wait_ge(pl_cp, 1)
                for g in range(NPG):
                    mm = pe.matmul(psS[:, g // 2, (g % 2) * S:(g % 2 + 1) * S], mixw[:, g, :], mT[:, g, :],
                                   start=True, stop=True)
                mm.then_inc(pl_mm, 1)
                pe.wait_ge(tok_ready, 1)
                tr_all(C, tokb)
                pe.wait_ge(tr_used, C.tr)
                for n in range(2):
                    slot, landed = C.next_slot()
                    pe.wait_ge(ld[slot], landed)
                    linear(C, xT, KC, ring[:, slot, :, :], UC)
                pe.wait_ge(pl_cp, 2)
                pe.wait_ge(s_poolw, 16)
                for n in range(2):
                    linear(C, mixT, 4, poolw[:, :, n * UC:(n + 1) * UC], UC)
                pe.wait_ge(merged_ready, 1)
                tr_all(C, xn)
                pe.wait_ge(tr_used, C.tr)
                for n in range(2):
                    slot, landed = C.next_slot()
                    pe.wait_ge(ld[slot], landed)
                    linear(C, xT, KC, ring[:, slot, :, :], UC)
                norm(C)
                pe.wait_ge(tr_used, C.tr)
                for t in range(NT):
                    for k in range(0, KC, 4):
                        tr_group(C, [xT[:, k + b, t * P:(t + 1) * P] for b in range(4)])
                pe.wait_ge(tr_used, C.tr)
                pe.wait_ge(lin_used, C.lin)

                for b in range(4):
                    mm = pe.matmul(lin[:, b, :], ident, cst("zero"), start=True, stop=False, skip_group_check=True)
                pe.sem_inc(v_free, V0)
                qbase = C.slot[0]

                def query(h, j, first):
                    wait_loop(pe, sk_ld[j], 16 * (1 if first else 1) if isinstance(h, int) and h < 2 else (h - j) * 8 + 16)
                    if not (isinstance(h, int) and h == 0):
                        wait_loop(pe, ps_used, h)
                        wait_loop(pe, q_used, h)
                        wait_loop(pe, sk_used, h)
                    for q in range(2):
                        for c in range(2):
                            mm = pe.transpose(psS[:, 0, (2 * q + c) * NKEY:(2 * q + c + 1) * NKEY],
                                              skn[:, j, q, c * P:(c + 1) * P], ident)
                    mm.then_inc(sk_done, 1)
                    wait_loop(pe, ld[j], (h - j) * 8 + 16 * (qbase + 1))
                    for b in range(4):
                        for k in range(KC):
                            mm = pe.matmul(psT[:, b // 2, (b % 2) * S:(b % 2 + 1) * S], ring[:, j, k, b * P:(b + 1) * P],
                                           xT[:, k, :], start=(k == 0), stop=(k == KC - 1))
                    mm.then_inc(q_done, 1)
                    wait_loop(pe, q_used, h + 1)
                    wait_loop(pe, sk_used, h + 1)
                    for t in range(NT):
                        for q in range(2):
                            for c in range(2):
                                mm = pe.matmul(psS[:, 1, (2 * t + q) * NKEY:(2 * t + q + 1) * NKEY],
                                               qTx[:, 2 * q + c, t * P:(t + 1) * P], skT[:, 2 * q + c, :],
                                               start=(c == 0), stop=(c == 1))
                    mm.then_inc(ps_done, 1)

                def expert_sum(h, j, t):
                    for k in range(TOPK):
                        n = 16 * (NT * j + t) + k
                        wait_loop(pe, dg_done, (h - j) * 32 + n + 1)
                        wait_loop(pe, v_ld[n % GB], l * LANDED + (h - j) * 64 + 16 * (n // GB + 1))
                        for half in range(2):
                            mm = pe.matmul(lin[:, 2 * half + t, :], diag[:, n % DB, :],
                                           vbuf[:, n % GB, half * 512:(half + 1) * 512], start=False, stop=False,
                                           skip_group_check=True)
                        mm.then_inc(v_free, 1)

                query(0, 0, True)
                with pe.Fori(0, PH // 2 - 1) as hp:
                    query(2 * hp + 1, 1, False)
                    for t in range(NT):
                        expert_sum(2 * hp, 0, t)
                    query(2 * hp + 2, 0, False)
                    for t in range(NT):
                        expert_sum(2 * hp + 1, 1, t)
                query(PH - 1, 1, False)
                for j in range(2):
                    for t in range(NT):
                        expert_sum(PH - 2 + j, j, t)
                for b in range(4):
                    mm = pe.matmul(lin[:, b, :], ident, cst("zero"), start=False, stop=True, skip_group_check=True)
                mm.then_inc(lin_done, 2)
                C.lin += 2
                layer_end(pe, l)

            C = Counts(RING2)
            pe.wait_ge(s_par, 128)
            pe.transpose(psT[:, 0, 0:64], prow[0:64, :], ident[0:64, 0:64]).then_inc(p_tr, 1)
            pe.wait_ge(p_col, 1)

            def three(out_ap, lhs, rhs, first, last):
                pe.matmul(out_ap, lhs[0], rhs[0], start=first, stop=False, skip_group_check=True)
                pe.matmul(out_ap, lhs[1], rhs[0], start=False, stop=False, skip_group_check=True)
                return pe.matmul(out_ap, lhs[0], rhs[1], start=False, stop=last, skip_group_check=True)

            def linear2(cols):
                pair = 2 * (C.lin % 2)
                if C.lin >= 2:
                    pe.wait_ge(lin_used, C.lin - 1)
                for p in range(NPC):
                    pe.wait_ge(lo_ready, NPC * C.unit + p + 1)
                    for t in range(NT):
                        for kk in range(2):
                            k = 2 * p + kk
                            tok = slice(t * P, (t + 1) * P)
                            w = [ws[:, p, q, kk * cols:(kk + 1) * cols] for q in range(2)]
                            mm = three(lin[:, pair + t, 0:cols], (xh[:, k, tok], xl[:, k, tok]), w,
                                       k == 0, k == KC - 1)
                    mm.then_inc(pc_used, 1)
                C.next_slot()
                C.lin += 1

            for i, m in enumerate(MIXERS2):
                norm(C)
                pe.wait_ge(tr_used, C.tr)
                n_in, cols = (NSWA, SWA_IN // NSWA) if m is SWA else (6, UC)
                for n in range(n_in):
                    linear2(cols)
                pe.wait_ge(qk_ready, i + 1)
                attention(C, m)
                pe.wait_ge(pt_copied, C.out)
                pe.wait_ge(pv_used, C.out)
                pe.wait_ge(tok_ready, i + 1)
                tr_all(C, tokb)
                pe.wait_ge(tr_used, C.tr)
                for n in range(2):
                    linear2(UC)
                norm(C)
                pe.wait_ge(tr_used, C.tr)
                pe.wait_ge(lin_used, C.lin)
                ub = i * 8
                for b in range(4):
                    pe.matmul(lin[:, b, 0:2], ident, cst("zero")[:, 0:2], start=True, stop=False, skip_group_check=True)

                def up(n, b, q0):
                    if not (isinstance(n, int) and n + ub < 2):
                        wait_loop(pe, rl_done, n + (ub - 1))
                    for p in range(NPC):
                        wait_loop(pe, lo_ready, q0 + (p + 1))
                        for k in range(KC):
                            w = [ws[:, p, q, k * P:(k + 1) * P] for q in range(2)]
                            mm = three((psT, psS)[b][:, p // 2, (p % 2) * S:(p % 2 + 1) * S], w,
                                       (xh[:, k, :], xl[:, k, :]), k == 0, k == KC - 1)
                        mm.then_inc(pc_used, 1)

                def down(n, b, q0, last=False):
                    wait_loop(pe, a_done, n + (ub + 1))
                    for p in range(NPC):
                        wait_loop(pe, lo_ready, q0 + (p + 1))
                        for t in range(NT):
                            a = [a_s[:, b, q, p * S + t * P:p * S + (t + 1) * P] for q in range(2)]
                            for half in range(2):
                                w = [ws[:, p, q, half * 512:(half + 1) * 512] for q in range(2)]
                                mm = three(lin[:, 2 * half + t, :], a, w, False, last and p == NPC - 1)
                        mm.then_inc(pc_used, 1)

                q = NPC * C.unit
                up(0, 0, q)
                up(1, 1, q + NPC)
                with pe.Fori(0, 3) as r:
                    down(2 * r, 0, 16 * r + (q + 2 * NPC))
                    up(2 * r + 2, 0, 16 * r + (q + 3 * NPC))
                    down(2 * r + 1, 1, 16 * r + (q + 4 * NPC))
                    up(2 * r + 3, 1, 16 * r + (q + 5 * NPC))
                down(6, 0, q + 14 * NPC)
                down(7, 1, q + 15 * NPC, last=True)
                C.unit += 16
                C.lin += 2

        @block.scalar
        def _(act):
            chain = [0]

            def link(ins):
                chain[0] += 1
                ins.then_inc(achain, 1)
                act.wait_ge(achain, chain[0])

            def norm(C):
                if C.x:
                    act.wait_ge(x_ready, C.x)
                n = C.norm
                for t in range(NT):
                    if t:
                        act.wait_ge(n_sq, 2 * n + 1)
                    elif n:
                        act.wait_ge(n_rstd, n)
                    act.activation(tokb[:, 0, :], x[:, t, :], ACT.Square, accum_out=st[:, t:t + 1]).then_inc(n_sq, 1)
                act.wait_ge(n_rec, n + 1)
                act.activation(st[:, 4:6], st[:, 2:4], ACT.Sqrt).then_inc(n_rstd, 1)
                C.norm += 1
                C.xn += 2

            def attention(C, m):
                for i in range(m.nsub + 2):
                    if i < m.nsub:
                        g = C.sc + i
                        act.wait_ge(sm_max, g + 1)
                        o = C.out + i // m.join
                        if m.join == 1:
                            if o >= 2:
                                act.wait_ge(pt_done, o - 1)
                        else:
                            if i >= 2:
                                act.wait_ge(pn_done, o)
                            if o >= 2 and i % 2 == 0:
                                act.wait_ge(pt_done, o - 1)
                        dst = pr if m.join == 1 else None
                        for t in range(NT):
                            if m.join == 1:
                                to = pr[:, g % 2, t, :]
                            else:
                                to = rope_t[:, 2 * (g % 2) + t, 0:S]
                            a = act.activation(to, sm[:, g % 2, t, :], ACT.Exp, bias=st[:, 12 + 2 * (g % 2) + t:13 + 2 * (g % 2) + t],
                                               accum_out=st[:, 16 + 2 * (g % 2) + t:17 + 2 * (g % 2) + t])
                        if m is SWA:
                            a = act.activation(st[:, 20 + 2 * (g % 2):22 + 2 * (g % 2)], st[:, 12 + 2 * (g % 2):14 + 2 * (g % 2)],
                                               ACT.Exp, bias=sinks[:, i:i + 1])
                        a.then_inc(ex_done, 1)
                    if m.head_at(i, 1) is not None:
                        g = C.out + m.head_at(i, 1)
                        act.wait_ge(pt_done, g + 1)
                        if g >= 2:
                            act.wait_ge(pv_done, g - 1)
                        act.activation(pT[:, g % 2, :, :].rearrange("p a s -> p (a s)"), psT[:, g % 2, :], ACT.Copy).then_inc(pt_copied, 1)
                C.sc += m.nsub
                C.out += m.nout

            act.wait_ge(s_const, 32)
            with act.Fori(0, DEPTH) as l:
                C = Counts()
                chain[0] = 0
                act.wait_ge(p_col, 1)
                act.activation(cact[:, :], pcol[:, 64:72], ACT.Silu).then_inc(s_cact, 1)
                norm(C)
                for n in range(8):
                    act.wait_ge(lin_done, C.lin + 1)
                    pair = 2 * (C.lin % 2)
                    a = act.activation(proj[:, :, n * UC:(n + 1) * UC], lin[:, pair:pair + 2, :],
                                       ACT.Copy if n < 4 else ACT.Sigmoid)
                    a.then_inc(lin_used, 1)
                    C.lin += 1
                    if n == 2:
                        act.wait_ge(hn_sq, 1)
                        act.activation(st[:, 44:64], st[:, 24:44], ACT.Sqrt).then_inc(hn_rs, 1)
                attention(C, GQA)
                act.wait_ge(pl_mm, 1)
                act.wait_ge(pv_done, C.out)
                act.activation(mT.rearrange("p a s -> p (a s)"), psS[:, :, :].rearrange("p b n -> p (b n)"), ACT.Copy).then_inc(pl_cp, 1)
                act.wait_ge(pl_mm, 2)
                act.wait_ge(pt_done, C.out)
                for g in range(NPG):
                    a = act.activation(mixT[:, g, :], psS[:, g // 2, (g % 2) * S:(g % 2 + 1) * S], ACT.Copy, scale=pcol[:, 72 + g:73 + g])
                a.then_inc(pl_cp, 1)
                C.x += 1
                act.wait_ge(tr_used, 4 + 5 + 4)
                norm(C)

                def query_copies(h):
                    if not (isinstance(h, int) and h == 0):
                        wait_loop(act, ps_done, h)
                    wait_loop(act, sk_done, h + 1)
                    act.activation(skT.rearrange("p a k -> p (a k)"), psS[:, 0, :], ACT.Copy).then_inc(sk_used, 1)
                    wait_loop(act, q_done, h + 1)
                    act.activation(qTx.rearrange("p a s -> p (a s)"), psT[:, :, :].rearrange("p b n -> p (b n)"), ACT.Copy).then_inc(q_used, 1)

                def expert_weights(h, j, t):
                    cb = NT * j + t
                    c = (h - j) * 2 + cb
                    wait_loop(act, idx_ready, c + 1)
                    act.activation(eg[:, cb, :], tops[:, cb, :], ACT.Exp, bias=nmx[:, cb, :],
                                   accum_out=ers[:, cb, 0:1]).then_inc(gate_ready, 1)
                    wait_loop(act, h_ready, c * 16 + 16)
                    act.activation(gel[:, cb, :], hdot[:, cb, :], ACT.Gelu).then_inc(gelu_ready, 1)
                    wait_loop(act, w_ready, c + 1)
                    for k in range(TOPK):
                        n = 16 * cb + k
                        wait_loop(act, v_free, (h - j) * 32 + (n + 1 - DB + V0))
                        act.activation(diag[:, n % DB, :], ident, ACT.Copy, scale=actw[:, cb, k:k + 1]).then_inc(dg_done, 1)

                query_copies(0)
                with act.Fori(0, PH // 2 - 1) as hp:
                    query_copies(2 * hp + 1)
                    for t in range(NT):
                        expert_weights(2 * hp, 0, t)
                    query_copies(2 * hp + 2)
                    for t in range(NT):
                        expert_weights(2 * hp + 1, 1, t)
                query_copies(PH - 1)
                for j in range(2):
                    for t in range(NT):
                        expert_weights(PH - 2 + j, j, t)
                layer_end(act, l)

            C = Counts(RING2)
            act.wait_ge(rope_arg, 1)
            act.activation(cs2[:, :, :, :].rearrange("p a t f -> p (a t f)"), ang[:, 4:6, :, :].rearrange("p a t f -> p (a t f)"), ACT.Sin).then_inc(rope_cs, 1)
            norm(C)
            C.x = 1

            def high_at(slot, landed, q0, kind, w, first=False):
                wait_loop(act, ld[slot], landed)
                for p in range(NPC):
                    if not first:
                        wait_loop(act, pc_used, q0 + (p + 1 - NPC))
                    act.activation(part(p, 0, kind, w), raw_piece(slot, p, kind, w), ACT.Copy).then_inc(hi_ready, 1)

            def high(kind="flat", w=D):
                q0 = NPC * C.unit
                slot, landed = C.next_slot()
                high_at(slot, landed, q0, kind, w, first=(q0 == 0))

            def xT_high(C, gains):
                for k in range(0, KC, 2):
                    act.wait_ge(tr_done, C.tr + 1)
                    if gains is None:
                        a = act.activation(xh[:, k:k + 2, :].rearrange("p k s -> p (k s)"), psT[:, C.tr % 2, :], ACT.Copy)
                    else:
                        for b in range(2):
                            a = act.activation(xh[:, k + b, :], psT[:, C.tr % 2, b * S:(b + 1) * S], ACT.Copy,
                                               scale=gains[:, k + b:k + b + 1])
                    a.then_inc(xh_ready, 1)
                    C.tr += 1

            for i, m in enumerate(MIXERS2):
                if m is DIFF:
                    act.wait_ge(lam_x, 3 * (i // 3) + 1)
                    act.activation(st[:, 8:10], st[:, 6:8], ACT.Exp).then_inc(lam_x, 1)
                n_in, w_in = (NSWA, 2 * SWA_IN // NSWA) if m is SWA else (6, D)
                high(w=w_in)
                norm(C)
                xT_high(C, pcol[:, 8 * i:8 * i + 8])
                for n in range(1, n_in + 1):
                    if n < n_in:
                        high(w=w_in)
                    if m is not SWA:
                        act.wait_ge(pc_used, NPC * (C.unit - (n < n_in)))
                        pair = 2 * (C.lin % 2)
                        act.activation(proj[:, :, (n - 1) * UC:n * UC], lin[:, pair:pair + 2, :], ACT.Copy).then_inc(lin_used, 1)
                    C.lin += 1
                high()
                C.tr += m.nblk // 2
                attention(C, m)
                if m is DIFF:
                    act.wait_ge(hn_sq, i // 3 + 1)
                    act.activation(st[:, 44:60], st[:, 24:40], ACT.Sqrt).then_inc(hn_rs, 1)
                xT_high(C, None)
                high()
                C.x += 1
                C.lin += 2
                high("block")
                norm(C)
                xT_high(C, pcol[:, 32 + 8 * i:40 + 8 * i])
                ub = i * 8

                def relu(n, b):
                    wait_loop(act, pc_used, (2 * n - 1) * NPC + (q + NPC) if not isinstance(n, int) else q + (NPC if n == 0 else 2 * n * NPC))
                    if not (isinstance(n, int) and n + ub < 2):
                        wait_loop(act, a_done, n + (ub - 1))
                    act.activation(rl(b), (psT, psS)[b][:, :, :].rearrange("p b n -> p (b n)"), ACT.Relu).then_inc(rl_done, 1)

                def act_high(n, b):
                    wait_loop(act, sq_done, n + (ub + 1))
                    act.activation(a_s[:, b, 0, :], rl(b), ACT.Copy).then_inc(ahi_done, 1)

                q = NPC * (C.unit - 1)
                high("block")
                relu(0, 0)
                act_high(0, 0)
                s2 = C.next_slot()
                s3 = C.next_slot()
                with act.Fori(0, 3) as r:
                    for b in range(2):
                        n = 2 * r + (b + 1)
                        landed = 32 * r + 16 * b
                        q0 = 16 * r + (q + (2 + 2 * b) * NPC)
                        high_at(s2[0], landed + s2[1], q0, "flat", D)
                        relu(n, 1 - b)
                        high_at(s3[0], landed + s3[1], q0 + NPC, "block", D)
                        act_high(n, 1 - b)
                for _ in range(10):
                    C.next_slot()
                high()
                relu(7, 1)
                high()
                act_high(7, 1)
                C.x += 1
                C.lin += 2
            norm(C)

        @block.vector
        def _(dve):
            chain = [0]

            def link(ins):
                chain[0] += 1
                ins.then_inc(dchain, 1)
                dve.wait_ge(dchain, chain[0])

            def restart_chain():
                dve.sem_clear(dchain)
                chain[0] = 0

            def norm(C, gain_row=None):
                n = C.norm
                dve.wait_ge(n_sq, 2 * n + 2)
                link(dve.tensor_scalar(st[:, 2:4], st[:, 0:2], 1.0 / D, EPS, ALU.mult, ALU.add))
                link(dve.reciprocal(st[:, 2:4], st[:, 2:4]))
                dve.sem_inc(n_rec, 1)
                dve.wait_ge(n_rstd, n + 1)
                for t in range(NT):
                    if gain_row is None:
                        dve.tensor_scalar(xn[:, t, :], x[:, t, :], st[:, 4 + t:5 + t], None, ALU.mult).then_inc(xn_ready, 1)
                    else:
                        to = gain_row[1]
                        link(dve.scalar_tensor_tensor(out=to[:, t, :], in0=x[:, t, :], scalar=st[:, 4 + t:5 + t], in1=gain_row[0],
                                                      op0=ALU.mult, op1=ALU.mult))
                C.norm += 1
                C.xn += 2

            def tr_copy(C, dst, scale=None, shift=None):
                dve.wait_ge(tr_done, C.tr + 1)
                for b in range(2):
                    src = psT[:, C.tr % 2, b * S:(b + 1) * S]
                    if scale is None:
                        ins = dve.tensor_copy(dst(b), src)
                    elif shift is None:
                        ins = dve.tensor_scalar(dst(b), src, scale(b), None, ALU.mult)
                    else:
                        ins = dve.tensor_scalar(dst(b), src, scale(b), shift(b), ALU.mult, ALU.add)
                ins.then_inc(tr_used, 1)
                C.tr += 1

            def tr_all(C, scale=None, shift=None):
                for k in range(0, KC, 2):
                    tr_copy(C, lambda b: xT[:, k + b, :],
                            None if scale is None else (lambda b: scale[:, k + b:k + b + 1]),
                            None if shift is None else (lambda b: shift[:, k + b:k + b + 1]))

            def residual(C, gates, used=None, between=None):
                for n in range(2):
                    if used is None:
                        dve.wait_ge(lin_done, C.lin + 1)
                    else:
                        if n and between:
                            between()
                        dve.wait_ge(pc_used, used[n])
                    pair = 2 * (C.lin % 2)
                    for t in range(NT):
                        xs = x[:, t, n * UC:(n + 1) * UC]
                        if gates is not None:
                            tmp = xn[:, t, n * UC:(n + 1) * UC]
                            link(dve.tensor_tensor(tmp, lin[:, pair + t, :], gates[:, n * UC:(n + 1) * UC], ALU.mult))
                            ins = dve.tensor_tensor(xs, xs, tmp, ALU.add)
                        else:
                            ins = dve.tensor_tensor(xs, xs, lin[:, pair + t, :], ALU.add)
                    ins.then_inc(lin_used, 1)
                    C.lin += 1
                dve.wait_ge(lin_used, C.lin)
                dve.sem_inc(x_ready, 1)
                C.x += 1

            def low_at(slot, q0, kind, w):
                for p in range(NPC):
                    wait_loop(dve, hi_ready, q0 + (p + 1))
                    dve.tensor_tensor(part(p, 1, kind, w), raw_piece(slot, p, kind, w), part(p, 0, kind, w).bitcast(F32),
                                      ALU.subtract).then_inc(lo_ready, 1)

            def low(C, kind="flat", w=D):
                q0 = NPC * C.unit
                slot, _ = C.next_slot()
                low_at(slot, q0, kind, w)

            def xT_low(C, gains):
                for k in range(0, KC, 2):
                    C.xh += 1
                    dve.wait_ge(xh_ready, C.xh)
                    if gains is None:
                        ins = dve.tensor_tensor(xl[:, k:k + 2, :].rearrange("p k s -> p (k s)"), psT[:, C.tr % 2, :],
                                                xh[:, k:k + 2, :].rearrange("p k s -> p (k s)").bitcast(F32), ALU.subtract)
                    else:
                        for b in range(2):
                            ins = dve.scalar_tensor_tensor(out=xl[:, k + b, :], in0=psT[:, C.tr % 2, b * S:(b + 1) * S],
                                                           scalar=gains[:, k + b:k + b + 1], in1=xh[:, k + b, :].bitcast(F32),
                                                           op0=ALU.mult, op1=ALU.subtract)
                    ins.then_inc(tr_used, 1)
                    C.tr += 1

            def attention(C, m):
                dve.wait_ge(qk_ready, 1)
                for b in range(0, m.nblk, 2):
                    if b < 8:
                        tr_copy(C, lambda c: qkT[:, b + c, :], lambda c: m.scale)
                    else:
                        tr_copy(C, lambda c: qkT[:, b + c, :])
                for i in range(m.nsub + 4):
                    if i < m.nsub:
                        g = C.sc + i
                        dve.wait_ge(sc_done, g + 1)
                        if g >= 2:
                            dve.wait_ge(ex_done, g - 1)
                        for t in range(NT):
                            mask = cst(m.mask)[:, t * S:(t + 1) * S]
                            ins = dve.tensor_tensor_reduce(sm[:, g % 2, t, :], psS[:, g % 2, t * S:(t + 1) * S], mask, 1.0, -3e38,
                                                           ALU.add, ALU.max, st[:, 10 + t:11 + t])
                        ins.then_inc(sc_used, 1)
                        dve.wait_ge(sc_used, g + 1)
                        nm = st[:, 12 + 2 * (g % 2):14 + 2 * (g % 2)]
                        if m is SWA:
                            ins = dve.tensor_scalar(nm, st[:, 10:12], sinks[:, i:i + 1], -1.0, ALU.max, ALU.mult)
                        else:
                            ins = dve.tensor_scalar(nm, st[:, 10:12], -1.0, None, ALU.mult)
                        ins.then_inc(sm_max, 1)
                        dve.wait_ge(sm_max, g + 1)
                    if 0 <= i - 1 < m.nsub:
                        probs(C, m, i - 1)
                    if m.head_at(i, 3) is not None:
                        heads(C, m, m.head_at(i, 3))
                C.sc += m.nsub
                C.out += m.nout

            def heads(C, m, o):
                g = C.out + o
                dve.wait_ge(pv_done, g + 1)
                dve.tensor_copy(tokb[:, :, o * m.width:(o + 1) * m.width],
                                lin[:, g % 2, 0:NT * m.width].rearrange("p (t w) -> p t w", t=NT)).then_inc(pv_used, 1)

            def probs(C, m, s):
                g = C.sc + s
                o = C.out + s // m.join
                dve.wait_ge(ex_done, g + 1)
                r = st[:, 16 + 2 * (g % 2):18 + 2 * (g % 2)]
                if m is SWA:
                    link(dve.tensor_tensor(r, r, st[:, 20 + 2 * (g % 2):22 + 2 * (g % 2)], ALU.add))
                link(dve.reciprocal(r, r))
                if m is DIFF and s % 2 == 1:
                    link(dve.tensor_scalar(r, r, st[:, 60:61], None, ALU.mult))
                for t in range(NT):
                    rt = st[:, 16 + 2 * (g % 2) + t:17 + 2 * (g % 2) + t]
                    if m is not DIFF:
                        ins = dve.tensor_scalar(pr[:, g % 2, t, :], pr[:, g % 2, t, :], rt, None, ALU.mult)
                    elif s % 2 == 0:
                        if t == 0 and o >= 2:
                            dve.wait_ge(pt_done, o - 1)
                        ins = dve.tensor_scalar(pr[:, o % 2, t, :], rope_t[:, 2 * (g % 2) + t, 0:S], rt, None, ALU.mult)
                    else:
                        ins = dve.scalar_tensor_tensor(out=pr[:, o % 2, t, :], in0=rope_t[:, 2 * (g % 2) + t, 0:S], scalar=rt,
                                                       in1=pr[:, o % 2, t, :], op0=ALU.mult, op1=ALU.add)
                if s % m.join == m.join - 1:
                    ins.then_inc(pn_done, 1)
                    dve.wait_ge(pn_done, o + 1)
                else:
                    link(ins)

            def head_rms(src, heads, lo, ready):
                for t in range(NT):
                    for name, (a, n) in enumerate(heads):
                        sq = xn[:, t, 0:n * P]
                        link(dve.tensor_tensor(sq, src[:, t, a:a + n * P], src[:, t, a:a + n * P], ALU.mult))
                        link(dve.tensor_reduce(st[:, lo:lo + n], sq.rearrange("p (h d) -> p h d", d=P), AX, ALU.add))
                        lo += n
                r = st[:, 24:lo]
                link(dve.tensor_scalar(r, r, 1.0 / P, EPS, ALU.mult, ALU.add))
                link(dve.reciprocal(r, r))
                dve.sem_inc(hn_sq, 1)
                dve.wait_ge(hn_rs, ready)

            dve.wait_ge(s_const, 32)
            dve.memset(base_f[:, :], 0.0).then_inc(pchain, 1)
            dve.wait_ge(pchain, 1)
            with dve.Fori(0, DEPTH) as l:
                C = Counts()
                chain[0] = 0
                dve.wait_ge(p_tr, 1)
                link(dve.memset(ones, 1.0))
                dve.tensor_copy(pcol[:, 0:76], psT[:, 0, 0:76]).then_inc(p_col, 1)
                dve.wait_ge(p_col, 1)
                dve.wait_ge(s_cact, 1)
                slots = Counts()
                for n in range(N_ADA * D // UC):
                    slot, landed = slots.next_slot()
                    dve.wait_ge(ld[slot], landed)
                    if n >= 2:
                        dve.wait_ge(s_ada, n - 1)
                    acc = ada_acc[:, n % 2, :]
                    link(dve.tensor_scalar(acc, ring[:, slot, 0, :], cact[:, 0:1], None, ALU.mult))
                    for k in range(1, KC):
                        ins = dve.scalar_tensor_tensor(out=acc, in0=ring[:, slot, k, :], scalar=cact[:, k:k + 1], in1=acc,
                                                       op0=ALU.mult, op1=ALU.add)
                        if k < KC - 1:
                            link(ins)
                    ins.then_inc(acc_ready, 1)
                dve.wait_ge(s_ada, 12)
                dve.wait_ge(s_par, 16 * 10)
                dve.tensor_tensor(rowb[:, :, :].rearrange("p a d -> p (a d)"), rowb[:, :, :].rearrange("p a d -> p (a d)"),
                                  lin[:, :, :].rearrange("p b n -> p (b n)"), ALU.add).then_inc(s_gbc, 1)
                dve.wait_ge(s_gbc, 1)
                for lo in (0, 24):
                    link(dve.tensor_tensor(modc[:, lo:lo + 16], psS[:, 0, lo:lo + 16], pcol[:, lo:lo + 16], ALU.add))
                for a, w, scl in ((0, 48, 8), (1, 56, 32)):
                    link(dve.tensor_scalar(aff[:, a, :], modc[:, scl:scl + 8], 1.0, None, ALU.add))
                    link(dve.tensor_tensor(aff[:, a, :], aff[:, a, :], pcol[:, w:w + 8], ALU.mult))
                norm(C)
                tr_all(C, aff[:, 0, :], modc[:, 0:8])
                dve.wait_ge(lin_used, 3)
                head_rms(proj, ((0, NQ1), (D, NKV1)), 24, 1)
                for t in range(NT):
                    for h in range(NQ1 + NKV1):
                        sl = proj[:, t, h * P:(h + 1) * P]
                        gain = wrow[:, 0 if h < NQ1 else 1, :]
                        ins = dve.scalar_tensor_tensor(out=sl, in0=sl, scalar=st[:, 44 + 10 * t + h:45 + 10 * t + h],
                                                       in1=gain, op0=ALU.mult, op1=ALU.mult)
                    link(ins)
                    nh = NQ1 + NKV1
                    v = proj[:, t, 0:nh * P].rearrange("p (h r e f) -> p h r e f", r=2, e=2, f=32)
                    tmp = xn[:, :, :].rearrange("p t d -> p (t d)")
                    for r in range(2):
                        x1, x2 = v[:, :, r, 0, :], v[:, :, r, 1, :]
                        w = nh * 32
                        co = cst("cos")[:, t * 64 + r * 32:t * 64 + (r + 1) * 32].rearrange("p (a f) -> p a f", a=1).to_broadcast([P, nh, 32])
                        si = cst("sin")[:, t * 64 + r * 32:t * 64 + (r + 1) * 32].rearrange("p (a f) -> p a f", a=1).to_broadcast([P, nh, 32])
                        tt = [tmp[:, q * w:(q + 1) * w].rearrange("p (h f) -> p h f", f=32) for q in range(4)]
                        dve.tensor_tensor(tt[0], x1, co, ALU.mult)
                        dve.tensor_tensor(tt[1], x2, si, ALU.mult)
                        dve.tensor_tensor(tt[2], x2, co, ALU.mult)
                        link(dve.tensor_tensor(tt[3], x1, si, ALU.mult))
                        dve.tensor_tensor(x1, tt[0], tt[1], ALU.subtract)
                        link(dve.tensor_tensor(x2, tt[2], tt[3], ALU.add))
                dve.sem_inc(qk_ready, 1)
                C.lin += 8
                dve.wait_ge(lin_used, C.lin)
                attention(C, GQA)
                dve.wait_ge(pv_used, C.out)
                dve.sem_inc(tok_ready, 1)
                tr_all(C)
                for n in range(4):
                    dve.wait_ge(lin_done, C.lin + 1)
                    pair = 2 * (C.lin % 2)
                    cols = slice((n % 2) * UC, (n % 2 + 1) * UC)
                    gc = (2048 if n < 2 else 3072) + (n % 2) * UC
                    for t in range(NT):
                        to = xn[:, t, cols] if n < 2 else tokb[:, t, cols]
                        link(dve.tensor_tensor(to, lin[:, pair + t, :], proj[:, t, gc:gc + UC], ALU.mult))
                    dve.sem_inc(lin_used, 1)
                    C.lin += 1
                link(dve.tensor_tensor(xn[:, :, :], xn[:, :, :], tokb[:, :, :], ALU.add))
                dve.sem_inc(merged_ready, 1)
                tr_all(C)
                residual(C, rowb[:, 0, :])
                norm(C)
                tr_all(C, aff[:, 1, :], modc[:, 24:32])
                for t in range(NT):
                    for k in range(0, KC, 4):
                        tr_copy(C, lambda b: tokb[:, t, (k + 2 * b) * P:(k + 2 * b + 2) * P])

                dve.sem_inc(u_free, GB)

                def top16(src, work, n, v, iu):
                    link(dve.max(v[:, 0:8], src))
                    link(dve.max_index(iu[:, 0:8], v[:, 0:8], src))
                    link(dve.match_replace(work, v[:, 0:8], src, -3e38))
                    link(dve.max(v[:, 8:16], work))
                    link(dve.max_index(iu[:, 8:16], v[:, 8:16], work))

                def topk(h, j, t):
                    cb = NT * j + t
                    restart_chain()
                    if t == 0:
                        wait_loop(dve, ps_done, h + 1)
                        link(dve.tensor_copy(topb[:, :, 0, :], psS[:, 1, :].rearrange("p (a n) -> p a n", n=NKEY)))
                        dve.sem_inc(ps_used, 1)
                    for q in range(2):
                        top16(topb[:, 2 * t + q, 0, :], topb[:, 2 * t + q, 1, :], NKEY, vals[:, q, :], idxu[:, q, :])
                    link(dve.tensor_copy(idxf[:, :, :], idxu[:, :, :]))
                    grid = [P, TOPK, TOPK]

                    def down(a):
                        return a.rearrange("p (a b) -> p a b", b=1).to_broadcast(grid)

                    def along(a):
                        return a.rearrange("p (a b) -> p a b", a=1).to_broadcast(grid)

                    def m(q):
                        return sc2[:, q, :].rearrange("p (a b) -> p a b", a=TOPK)

                    link(dve.tensor_tensor(m(0), down(vals[:, 0, :]), along(vals[:, 1, :]), ALU.add))
                    if not (isinstance(h, int) and h < 2):
                        wait_loop(dve, v_free, h * 32 + (16 * t + 16 + V0 - 64), alone=True)
                    top16(sc2[:, 0, :], sc2[:, 1, :], 256, tops[:, cb, :], posu[:, 0, :])
                    link(dve.tensor_scalar(nmx[:, cb, :], tops[:, cb, 0:1], -1.0, None, ALU.mult))
                    link(dve.tensor_scalar(posu[:, 1, :], posu[:, 0, :], 4, None, ALU.logical_shift_right))
                    link(dve.tensor_scalar(posu[:, 2, :], posu[:, 0, :], 15, None, ALU.bitwise_and))
                    link(dve.tensor_copy(posfl[:, 0:2, :], posu[:, 1:3, :]))
                    for q in range(2):
                        link(dve.tensor_tensor(m(2 + q), down(posfl[:, q, :]), along(cst("iota")), ALU.is_equal))
                        link(dve.tensor_tensor(m(4 + q), m(2 + q), along(idxf[:, q, :]), ALU.mult))
                        link(dve.tensor_reduce(posfl[:, 2 + q, :], m(4 + q), AX, ALU.add))
                    link(dve.scalar_tensor_tensor(out=posfl[:, 0, :], in0=posfl[:, 2, :], scalar=float(NKEY), in1=posfl[:, 3, :],
                                                  op0=ALU.mult, op1=ALU.add))
                    link(dve.tensor_scalar(eidx[:, cb, :], posfl[:, 0, :], base_f[:, 0:1], None, ALU.add))
                    dve.sem_inc(idx_ready, 1)

                def dots(h, j, t):
                    cb = NT * j + t
                    c = (h - j) * 2 + cb
                    for k in range(TOPK):
                        n = 16 * cb + k
                        wait_loop(dve, u_ld[n % GB], l * LANDED + (h - j) * 64 + 16 * (n // GB + 1))
                        dve.tensor_tensor_reduce(ubuf[:, n % GB, :], ubuf[:, n % GB, :], tokb[:, t, :], 1.0, 0.0,
                                                 ALU.mult, ALU.add, hdot[:, cb, k:k + 1]).then_inc(h_ready, 1)
                    wait_loop(dve, gate_ready, c + 1, alone=True)
                    restart_chain()
                    link(dve.reciprocal(ers[:, cb, 1:2], ers[:, cb, 0:1]))
                    wait_loop(dve, gelu_ready, c + 1)
                    link(dve.scalar_tensor_tensor(out=actw[:, cb, :], in0=eg[:, cb, :], scalar=ers[:, cb, 1:2], in1=gel[:, cb, :],
                                                  op0=ALU.mult, op1=ALU.mult))
                    dve.sem_inc(w_ready, 1)

                for t in range(NT):
                    topk(0, 0, t)
                with dve.Fori(0, PH // 2 - 1) as hp:
                    for j in range(2):
                        for t in range(NT):
                            dots(2 * hp + j, j, t)
                            topk(2 * hp + j + 1, 1 - j, t)
                for t in range(NT):
                    dots(PH - 2, 0, t)
                    topk(PH - 1, 1, t)
                for t in range(NT):
                    dots(PH - 1, 1, t)
                restart_chain()
                link(dve.tensor_scalar(base_f[:, :], base_f[:, :], float(NEXP), None, ALU.add))
                residual(C, rowb[:, 1, :])
                layer_end(dve, l)

            C = Counts(RING2)
            chain[0] = 0
            dve.wait_ge(s_par, 128)
            dve.wait_ge(p_tr, 1)
            dve.tensor_copy(pcol[:, 0:64], psT[:, 0, 0:64]).then_inc(p_col, 1)
            link(dve.tensor_copy(posf[:, :], posi[:, :]))
            for t in range(NT):
                ins = dve.tensor_scalar(ang[:, 0, t, :], cst("inv"), posf[:, t:t + 1], None, ALU.mult)
            link(ins)
            TWO_PI = 2.0 * np.pi
            PARTS = [6.28125, float(np.float32(TWO_PI - 6.28125).view(np.uint32) & np.uint32(0xFFFFF000)) * 0]
            c1 = 6.28125
            c2 = float(np.array(np.array([TWO_PI - c1], np.float32).view(np.uint32) & np.uint32(0xFFFFF000)).view(np.float32)[0])
            c3 = float(np.float32(TWO_PI - c1 - c2))
            ROUND = 12582912.0
            for q, quarter in ((0, 0.25), (1, 0.0)):
                a, k, r = ang[:, 0, :, :], ang[:, 1, :, :], ang[:, 4 + q, :, :]
                link(dve.tensor_scalar(k, a, 1.0 / TWO_PI, quarter, ALU.mult, ALU.add))
                link(dve.tensor_scalar(k, k, ROUND, None, ALU.add))
                link(dve.tensor_scalar(k, k, -ROUND, None, ALU.add))
                link(dve.scalar_tensor_tensor(out=r, in0=k, scalar=-c1, in1=a, op0=ALU.mult, op1=ALU.add))
                link(dve.scalar_tensor_tensor(out=r, in0=k, scalar=-c2, in1=r, op0=ALU.mult, op1=ALU.add))
                link(dve.scalar_tensor_tensor(out=r, in0=k, scalar=-c3, in1=r, op0=ALU.mult, op1=ALU.add))
                if quarter:
                    link(dve.tensor_scalar(r, r, float(np.pi / 2), None, ALU.add))
                link(dve.tensor_scalar(r, r, 3.1415925, -3.1415925, ALU.min, ALU.max))
            dve.sem_inc(rope_arg, 1)
            norm(C, (rowb[:, 0, :], x))
            dve.sem_inc(x_ready, 1)
            C.xn = 0
            C.x = 1
            dve.wait_ge(rope_cs, 1)
            for i, m in enumerate(MIXERS2):
                slot = i // 3
                if m is DIFF:
                    dve.wait_ge(lam_e, 64 * (slot + 1))
                    for q in range(2):
                        link(dve.tensor_tensor_reduce(lamv[:, 2 * q, :], lamv[:, 2 * q, :], lamv[:, 2 * q + 1, :], 1.0, 0.0,
                                                      ALU.mult, ALU.add, st[:, 6 + q:7 + q]))
                    dve.sem_inc(lam_x, 1)
                    dve.wait_ge(lam_x, 3 * slot + 2)
                    link(dve.tensor_tensor(st[:, 60:61], st[:, 9:10], st[:, 8:9], ALU.subtract))
                    link(dve.tensor_scalar(st[:, 60:61], st[:, 60:61], -LAM_INIT[i], None, ALU.add))
                    dve.sem_inc(lam_x, 1)
                low(C, w=2 * SWA_IN // NSWA if m is SWA else D)
                norm(C)
                xT_low(C, pcol[:, 8 * i:8 * i + 8])
                if m is SWA:
                    w = SWA_IN // NSWA
                    for n in range(NSWA):
                        if n < NSWA - 1:
                            low(C, w=2 * w)
                        dve.wait_ge(pc_used, NPC * (C.unit - (n < NSWA - 1)))
                        pair = 2 * (C.lin % 2)
                        for t in range(NT):
                            ins = dve.tensor_tensor(proj[:, t, n * w:(n + 1) * w], lin[:, pair + t, 0:w], bias_row[:, n * w:(n + 1) * w], ALU.add)
                        link(ins)
                        dve.sem_inc(lin_used, 1)
                        C.lin += 1
                    nh = 18
                else:
                    for n in range(5):
                        low(C)
                    dve.wait_ge(lin_used, C.lin + 4)
                    C.lin += 6
                    nh = 32
                for t in range(NT):
                    v = proj[:, t, 0:nh * HD2].rearrange("p (h d) -> p h d", d=HD2)
                    x1, x2 = v[:, :, 0:8], v[:, :, 8:16]
                    co = cs2[:, 0, t, :].rearrange("p (a f) -> p a f", a=1).to_broadcast([P, nh, 8])
                    si = cs2[:, 1, t, :].rearrange("p (a f) -> p a f", a=1).to_broadcast([P, nh, 8])
                    tt = [rope_t[:, q, 0:nh * 8].rearrange("p (h f) -> p h f", f=8) for q in range(4)]
                    dve.tensor_tensor(tt[0], x1, co, ALU.mult)
                    dve.tensor_tensor(tt[1], x2, si, ALU.mult)
                    dve.tensor_tensor(tt[2], x2, co, ALU.mult)
                    link(dve.tensor_tensor(tt[3], x1, si, ALU.mult))
                    dve.tensor_tensor(x1, tt[0], tt[1], ALU.subtract)
                    link(dve.tensor_tensor(x2, tt[2], tt[3], ALU.add))
                if m is SWA:
                    for t in range(NT):
                        k3 = proj[:, t, D:D + 2 * HD2].rearrange("p (h d) -> p h d", d=HD2)
                        d3 = xn[:, t, 0:2 * P].rearrange("p (h r d) -> p h r d", r=2, d=HD2)
                        dve.tensor_copy(d3[:, :, 0, :], k3)
                        ins = dve.tensor_copy(d3[:, :, 1, :], k3)
                    link(ins)
                dve.sem_inc(qk_ready, 1)
                low(C)
                attention(C, m)
                dve.wait_ge(pv_used, C.out)
                if m is DIFF:
                    head_rms(tokb, ((0, 8),), 24, slot + 1)
                    for t in range(NT):
                        for h in range(8):
                            sl = tokb[:, t, h * P:(h + 1) * P]
                            ins = dve.scalar_tensor_tensor(out=sl, in0=sl, scalar=st[:, 44 + 8 * t + h:45 + 8 * t + h],
                                                           in1=wrow[:, slot, :], op0=ALU.mult, op1=ALU.mult)
                    link(ins)
                    link(dve.tensor_scalar(tokb[:, :, :], tokb[:, :, :], 1.0 - LAM_INIT[i], None, ALU.mult))
                dve.sem_inc(tok_ready, 1)
                xT_low(C, None)
                low(C)
                u = C.unit
                residual(C, None, (NPC * (u - 1), NPC * u), lambda: low(C, "block"))
                norm(C)
                xT_low(C, pcol[:, 32 + 8 * i:40 + 8 * i])
                ub = i * 8

                def square(n, b):
                    wait_loop(dve, rl_done, n + (ub + 1))
                    dve.tensor_tensor(rl(b), rl(b), rl(b), ALU.mult).then_inc(sq_done, 1)

                def act_low(n, b):
                    wait_loop(dve, ahi_done, n + (ub + 1))
                    dve.tensor_tensor(a_s[:, b, 1, :], rl(b), a_s[:, b, 0, :].bitcast(F32), ALU.subtract).then_inc(a_done, 1)

                q = NPC * (C.unit - 1)
                low(C, "block")
                square(0, 0)
                act_low(0, 0)
                s2 = C.next_slot()
                s3 = C.next_slot()
                with dve.Fori(0, 3) as r:
                    for b in range(2):
                        n = 2 * r + (b + 1)
                        q0 = 16 * r + (q + (2 + 2 * b) * NPC)
                        low_at(s2[0], q0, "flat", D)
                        square(n, 1 - b)
                        low_at(s3[0], q0 + NPC, "block", D)
                        act_low(n, 1 - b)
                for _ in range(10):
                    C.next_slot()
                low(C)
                square(7, 1)
                low(C)
                act_low(7, 1)
                residual(C, None, (NPC * C.unit, NPC * C.unit))
            norm(C, (rowb[:, 1, :], xn))
            dve.sem_inc(xn_ready, 2)

        @block.gpsimd
        def _(pool):
            table = {"u": T["expert_u"].rearrange("l e d -> (l e) d"), "v": T["expert_v"].rearrange("l e d -> (l e) d")}
            with pool.Fori(0, DEPTH) as l:
                def gathers(hbase, j, t):
                    cb = NT * j + t
                    wait_loop(pool, idx_ready, hbase * 2 + cb + 1)
                    for which, buf, landed, in_use, credit in (("u", ubuf, u_ld, h_ready, u_free), ("v", vbuf, v_ld, v_free, None)):
                        for k in range(TOPK):
                            n = 16 * cb + k
                            if credit is None:
                                wait_loop(pool, in_use, hbase * 32 + (n + 1 + V0 - GB), alone=True)
                            elif isinstance(hbase, int) and hbase == 0:
                                if n >= GB:
                                    pool.wait_ge(in_use, n - GB + 1)
                            else:
                                wait_loop(pool, in_use, hbase * 32 + (n - GB + 1), alone=True)
                            pool.indirect_dma_start(
                                out=buf[:, n % GB, :], out_offset=None, in_=table[which],
                                in_offset=bass.IndirectOffsetOnAxis(ap=eidx[:, cb, k:k + 1], axis=0),
                            ).then_inc(landed[n % GB], 16)

                for j in range(2):
                    for t in range(NT):
                        gathers(0, j, t)
                with pool.Fori(1, PH // 2) as hp:
                    for j in range(2):
                        for t in range(NT):
                            gathers(2 * hp, j, t)
                layer_end(pool, l)


def kernel(**inputs):
    import concourse.bacc as _bacc
    from concourse.bass_utils import run_bass_kernel_spmd as _run

    nc = _bacc.Bacc("TRN2", target_bir_lowering=False, num_devices=1)
    arrays, tensors = {}, {}
    for name in INS1 + INS2:
        a = np.ascontiguousarray(inputs[name])
        arrays[f"in_{name}"] = a
        tensors[name] = nc.dram_tensor(f"in_{name}", a.shape, mybir.dt.from_np(a.dtype), kind="ExternalInput").ap()
    arrays["in_consts"] = const_table()
    tensors["consts"] = nc.dram_tensor("in_consts", (P, CW), F32, kind="ExternalInput").ap()
    out = nc.dram_tensor("out_0", (1, S, D), F32, kind="ExternalOutput").ap()
    program(nc, tensors, out)
    r = _run(nc, [arrays], core_ids=[0])
    return r.results[0]["out_0"]
```
